# Optimizing a Trainium2 kernel written in Bass

```python
import jax, jax.numpy as jnp
from jax import lax
import numpy as np

D_MODEL = 1024
BATCH = 1
SEQ = 256
DEPTH = 1
DEC_BATCH = 1
DEC_SEQ = 64
PAST_LEN = 512

CHUNK = 64
HEAD_DIM = 64
N_HEADS_FOX = 8
N_HEADS_BAND = 8
W_FOX = N_HEADS_FOX * HEAD_DIM
W_BAND = N_HEADS_BAND * HEAD_DIM
MIX_WIDTH = W_FOX + W_BAND
PROJ_COLS = 3 * W_FOX + 3 * W_BAND + N_HEADS_FOX
LEFT_CHUNKS = 8
LEFT = LEFT_CHUNKS * CHUNK
BAND = (LEFT_CHUNKS + 1) * CHUNK
REL_CLIP = 128
N_MEM = 256
N_HEADS_MEM = 4
HEAD_DIM_MEM = 128
W_MEM = N_HEADS_MEM * HEAD_DIM_MEM
N_GROUPS = 4
EXPERTS_PER_GROUP = 8
N_EXPERTS = N_GROUPS * EXPERTS_PER_GROUP
TOP_K_INNER = 2
D_EXPERT = 512
Q_BLOCK = 128
EPS = 1e-6
NEG_INF = -1e30
FORGET_BIAS_INIT = 4.0
ATTN_SCALE = HEAD_DIM ** -0.5
MEM_SCALE = HEAD_DIM_MEM ** -0.5

kernel_name = "fox_band_hier_moe_stream_step"

def rmsnorm(x, g):
    xf = x.astype(jnp.float32)
    y = xf * lax.rsqrt(jnp.mean(xf * xf, axis=-1, keepdims=True) + EPS)
    return (y * g.astype(jnp.float32)).astype(x.dtype)

def mixer_proj(h, w_in, b_f):
    z = jnp.einsum('bsd,de->bse', h, w_in)
    B, S, _ = z.shape
    idx = [W_FOX, 2 * W_FOX, 3 * W_FOX, 3 * W_FOX + W_BAND, 3 * W_FOX + 2 * W_BAND, 3 * W_FOX + 3 * W_BAND]
    qa, ka, va, qb, kb, vb, fl = jnp.split(z, idx, axis=-1)
    hd = lambda t, n: t.reshape(B, S, n, HEAD_DIM)
    logf = jax.nn.log_sigmoid(fl.astype(jnp.float32) + b_f.astype(jnp.float32))
    return (hd(qa, N_HEADS_FOX), hd(ka, N_HEADS_FOX), hd(va, N_HEADS_FOX),
            hd(qb, N_HEADS_BAND), hd(kb, N_HEADS_BAND), hd(vb, N_HEADS_BAND), logf)

def fox_prompt(q, k, v, logf):
    B, S, H, Dh = q.shape
    nb = S // Q_BLOCK
    c = jnp.cumsum(logf, axis=1)
    cT = c.transpose(0, 2, 1)
    qb = q.reshape(B, nb, Q_BLOCK, H, Dh).transpose(1, 0, 2, 3, 4)
    cb = c.reshape(B, nb, Q_BLOCK, H).transpose(1, 0, 3, 2)
    pos_k = jnp.arange(S)

    def block(args):
        qi, ci, bi = args
        s = jnp.einsum('bqhd,bkhd->bhqk', qi, k).astype(jnp.float32) * ATTN_SCALE
        s = s + ci[..., None] - cT[:, :, None, :]
        pos_q = bi * Q_BLOCK + jnp.arange(Q_BLOCK)
        s = jnp.where(pos_k[None, :] <= pos_q[:, None], s, NEG_INF)
        p = jax.nn.softmax(s, axis=-1).astype(v.dtype)
        return jnp.einsum('bhqk,bkhd->bqhd', p, v)

    out = lax.map(block, (qb, cb, jnp.arange(nb)))
    return out.transpose(1, 0, 2, 3, 4).reshape(B, S, H, Dh)

def fox_sample(q, k, v, logf, ck, cv, clogf):
    P = ck.shape[1]
    T = q.shape[1]
    k_all = jnp.concatenate([ck, k], axis=1)
    v_all = jnp.concatenate([cv, v], axis=1)
    c = jnp.cumsum(jnp.concatenate([clogf.astype(jnp.float32), logf], axis=1), axis=1)
    cT = c.transpose(0, 2, 1)
    s = jnp.einsum('bqhd,bkhd->bhqk', q, k_all).astype(jnp.float32) * ATTN_SCALE
    s = s + cT[:, :, P:, None] - cT[:, :, None, :]
    mask = jnp.arange(P + T)[None, :] <= P + jnp.arange(T)[:, None]
    s = jnp.where(mask, s, NEG_INF)
    p = jax.nn.softmax(s, axis=-1).astype(v_all.dtype)
    return jnp.einsum('bhqk,bkhd->bqhd', p, v_all)

def rel_bias(table, rel):
    idx = jnp.clip(rel, -REL_CLIP, REL_CLIP) + REL_CLIP
    return table[idx].transpose(2, 0, 1).astype(jnp.float32)

def band_prompt(q, k, v, table):
    B, S, H, Dh = q.shape
    nc = S // CHUNK
    pad = ((0, 0), (LEFT, 0), (0, 0), (0, 0))
    kp = jnp.pad(k, pad).reshape(B, nc + LEFT_CHUNKS, CHUNK, H, Dh)
    vp = jnp.pad(v, pad).reshape(B, nc + LEFT_CHUNKS, CHUNK, H, Dh)
    kb = jnp.concatenate([kp[:, j:j + nc] for j in range(LEFT_CHUNKS + 1)], axis=2)
    vb = jnp.concatenate([vp[:, j:j + nc] for j in range(LEFT_CHUNKS + 1)], axis=2)
    qc = q.reshape(B, nc, CHUNK, H, Dh)
    s = jnp.einsum('bnqhd,bnkhd->bnhqk', qc, kb).astype(jnp.float32) * ATTN_SCALE
    rel = jnp.arange(CHUNK)[:, None] + LEFT - jnp.arange(BAND)[None, :]
    s = s + rel_bias(table, rel)[None, None]
    key_pos = (jnp.arange(nc)[:, None] - LEFT_CHUNKS) * CHUNK + jnp.arange(BAND)[None, :]
    s = jnp.where((key_pos >= 0)[None, :, None, None, :], s, NEG_INF)
    p = jax.nn.softmax(s, axis=-1).astype(vb.dtype)
    return jnp.einsum('bnhqk,bnkhd->bnqhd', p, vb).reshape(B, S, H, Dh)

def band_sample(q, k, v, ck, cv, table):
    BP = ck.shape[1]
    T = q.shape[1]
    k_all = jnp.concatenate([ck, k], axis=1)
    v_all = jnp.concatenate([cv, v], axis=1)
    s = jnp.einsum('bqhd,bkhd->bhqk', q, k_all).astype(jnp.float32) * ATTN_SCALE
    rel = jnp.arange(T)[:, None] + BP - jnp.arange(BP + T)[None, :]
    s = s + rel_bias(table, rel)[None]
    p = jax.nn.softmax(s, axis=-1).astype(v_all.dtype)
    o = jnp.einsum('bhqk,bkhd->bqhd', p, v_all)
    return o, k_all[:, T:], v_all[:, T:]

def merge_groups(o_fox, o_band, g_of, g_ob, w_out):
    B, S = o_fox.shape[:2]
    a = rmsnorm(o_fox.reshape(B, S, W_FOX), g_of)
    b = rmsnorm(o_band.reshape(B, S, W_BAND), g_ob)
    return jnp.einsum('bse,ed->bsd', jnp.concatenate([a, b], axis=-1), w_out)

def mem_kv(mem, g_mem, w_ck, w_cv):
    B = mem.shape[0]
    m = rmsnorm(mem, g_mem)
    mk = jnp.einsum('bmd,de->bme', m, w_ck).reshape(B, -1, N_HEADS_MEM, HEAD_DIM_MEM)
    mv = jnp.einsum('bmd,de->bme', m, w_cv).reshape(B, -1, N_HEADS_MEM, HEAD_DIM_MEM)
    return mk, mv

def cross_attn(h, mk, mv, w_cq, w_co):
    B, S, _ = h.shape
    q = jnp.einsum('bsd,de->bse', h, w_cq).reshape(B, S, N_HEADS_MEM, HEAD_DIM_MEM)
    s = jnp.einsum('bqhd,bmhd->bhqm', q, mk).astype(jnp.float32) * MEM_SCALE
    p = jax.nn.softmax(s, axis=-1).astype(mv.dtype)
    o = jnp.einsum('bhqm,bmhd->bqhd', p, mv).reshape(B, S, W_MEM)
    return jnp.einsum('bse,ed->bsd', o, w_co)

def hier_moe(h, w_r1, b_r1, w_r2, b_r2, w_g, w_u, w_d):
    B, S, Dm = h.shape
    x = h.reshape(B * S, Dm)
    l1 = jnp.einsum('td,dg->tg', x, w_r1).astype(jnp.float32) + b_r1.astype(jnp.float32)
    p1 = jax.nn.softmax(l1, axis=-1)
    grp = jnp.argmax(l1, axis=-1)
    wg = jnp.take_along_axis(p1, grp[:, None], axis=-1)[:, 0]
    l2 = (jnp.einsum('td,de->te', x, w_r2).astype(jnp.float32) + b_r2.astype(jnp.float32))
    l2 = l2.reshape(-1, N_GROUPS, EXPERTS_PER_GROUP)
    l2g = jnp.take_along_axis(l2, grp[:, None, None], axis=1)[:, 0]
    top_v, top_i = lax.top_k(jax.nn.softmax(l2g, axis=-1), TOP_K_INNER)
    top_v = top_v / jnp.sum(top_v, axis=-1, keepdims=True)
    eid = grp[:, None] * EXPERTS_PER_GROUP + top_i
    gate = jnp.sum(jax.nn.one_hot(eid, N_EXPERTS, dtype=jnp.float32)
                   * (wg[:, None] * top_v)[..., None], axis=1)
    y = jnp.zeros((B * S, Dm), jnp.float32)
    for e in range(N_EXPERTS):
        a = jax.nn.silu(x @ w_g[e]) * (x @ w_u[e])
        y = y + gate[:, e:e + 1] * (a @ w_d[e]).astype(jnp.float32)
    return y.astype(h.dtype).reshape(B, S, Dm)

def setup_inputs(seed: int = 0) -> dict:
    key = jax.random.key(seed)
    ks = iter(jax.random.split(key, 40))
    nrm = lambda shape, s=1.0: s * jax.random.normal(next(ks), shape, jnp.float32)
    gain = lambda shape: 1.0 + nrm(shape, 0.02)
    bp = min(LEFT, PAST_LEN)
    return {
        "x_prompt": nrm((BATCH, SEQ, D_MODEL)),
        "x_sample": nrm((DEC_BATCH, DEC_SEQ, D_MODEL)),
        "cache_fox_k": nrm((DEPTH, DEC_BATCH, PAST_LEN, N_HEADS_FOX, HEAD_DIM)),
        "cache_fox_v": nrm((DEPTH, DEC_BATCH, PAST_LEN, N_HEADS_FOX, HEAD_DIM)),
        "cache_fox_logf": jax.nn.log_sigmoid(FORGET_BIAS_INIT + nrm((DEPTH, DEC_BATCH, PAST_LEN, N_HEADS_FOX), 0.5)),
        "cache_band_k": nrm((DEPTH, DEC_BATCH, bp, N_HEADS_BAND, HEAD_DIM)),
        "cache_band_v": nrm((DEPTH, DEC_BATCH, bp, N_HEADS_BAND, HEAD_DIM)),
        "cache_mem_k": nrm((DEPTH, DEC_BATCH, N_MEM, N_HEADS_MEM, HEAD_DIM_MEM)),
        "cache_mem_v": nrm((DEPTH, DEC_BATCH, N_MEM, N_HEADS_MEM, HEAD_DIM_MEM)),
        "mem_prompt": nrm((BATCH, N_MEM, D_MODEL)),
        "g_mix": gain((DEPTH, D_MODEL)),
        "w_in": nrm((DEPTH, D_MODEL, PROJ_COLS), D_MODEL ** -0.5),
        "b_forget": FORGET_BIAS_INIT + nrm((DEPTH, N_HEADS_FOX), 0.5),
        "g_out_fox": gain((DEPTH, W_FOX)),
        "g_out_band": gain((DEPTH, W_BAND)),
        "rel_table": nrm((DEPTH, 2 * REL_CLIP + 1, N_HEADS_BAND), 0.2),
        "w_out": nrm((DEPTH, MIX_WIDTH, D_MODEL), MIX_WIDTH ** -0.5),
        "g_cross": gain((DEPTH, D_MODEL)),
        "g_mem": gain((DEPTH, D_MODEL)),
        "w_cq": nrm((DEPTH, D_MODEL, W_MEM), D_MODEL ** -0.5),
        "w_ck": nrm((DEPTH, D_MODEL, W_MEM), D_MODEL ** -0.5),
        "w_cv": nrm((DEPTH, D_MODEL, W_MEM), D_MODEL ** -0.5),
        "w_co": nrm((DEPTH, W_MEM, D_MODEL), W_MEM ** -0.5),
        "g_ffn": gain((DEPTH, D_MODEL)),
        "w_router1": nrm((DEPTH, D_MODEL, N_GROUPS), D_MODEL ** -0.5),
        "b_router1": nrm((DEPTH, N_GROUPS), 0.01),
        "w_router2": nrm((DEPTH, D_MODEL, N_EXPERTS), D_MODEL ** -0.5),
        "b_router2": nrm((DEPTH, N_EXPERTS), 0.01),
        "w_exp_gate": nrm((DEPTH, N_EXPERTS, D_MODEL, D_EXPERT), D_MODEL ** -0.5),
        "w_exp_up": nrm((DEPTH, N_EXPERTS, D_MODEL, D_EXPERT), D_MODEL ** -0.5),
        "w_exp_down": nrm((DEPTH, N_EXPERTS, D_EXPERT, D_MODEL), D_EXPERT ** -0.5),
        "g_final": gain((D_MODEL,)),
    }

def reference(x_prompt, x_sample, cache_fox_k, cache_fox_v, cache_fox_logf, cache_band_k, cache_band_v,
              cache_mem_k, cache_mem_v, mem_prompt, g_mix, w_in, b_forget, g_out_fox, g_out_band, rel_table,
              w_out, g_cross, g_mem, w_cq, w_ck, w_cv, w_co, g_ffn, w_router1, b_router1, w_router2,
              b_router2, w_exp_gate, w_exp_up, w_exp_down, g_final):
    xp, xs = x_prompt, x_sample
    fkp, fvp, flp, bkp, bvp, mkp, mvp = [], [], [], [], [], [], []
    fks, fvs, fls, bks, bvs = [], [], [], [], []
    for l in range(DEPTH):
        h = rmsnorm(xp, g_mix[l])
        qa, ka, va, qb, kb, vb, lf = mixer_proj(h, w_in[l], b_forget[l])
        oa = fox_prompt(qa, ka, va, lf)
        ob = band_prompt(qb, kb, vb, rel_table[l])
        xp = xp + merge_groups(oa, ob, g_out_fox[l], g_out_band[l], w_out[l])
        mk, mv = mem_kv(mem_prompt, g_mem[l], w_ck[l], w_cv[l])
        xp = xp + cross_attn(rmsnorm(xp, g_cross[l]), mk, mv, w_cq[l], w_co[l])
        xp = xp + hier_moe(rmsnorm(xp, g_ffn[l]), w_router1[l], b_router1[l], w_router2[l], b_router2[l],
                           w_exp_gate[l], w_exp_up[l], w_exp_down[l])
        nkeep = min(LEFT, kb.shape[1])
        fkp.append(ka); fvp.append(va); flp.append(lf)
        bkp.append(kb[:, kb.shape[1] - nkeep:]); bvp.append(vb[:, vb.shape[1] - nkeep:])
        mkp.append(mk); mvp.append(mv)
        h = rmsnorm(xs, g_mix[l])
        qa, ka, va, qb, kb, vb, lf = mixer_proj(h, w_in[l], b_forget[l])
        oa = fox_sample(qa, ka, va, lf, cache_fox_k[l], cache_fox_v[l], cache_fox_logf[l])
        ob, nbk, nbv = band_sample(qb, kb, vb, cache_band_k[l], cache_band_v[l], rel_table[l])
        xs = xs + merge_groups(oa, ob, g_out_fox[l], g_out_band[l], w_out[l])
        xs = xs + cross_attn(rmsnorm(xs, g_cross[l]), cache_mem_k[l], cache_mem_v[l], w_cq[l], w_co[l])
        xs = xs + hier_moe(rmsnorm(xs, g_ffn[l]), w_router1[l], b_router1[l], w_router2[l], b_router2[l],
                           w_exp_gate[l], w_exp_up[l], w_exp_down[l])
        fks.append(ka); fvs.append(va); fls.append(lf.astype(cache_fox_logf.dtype))
        bks.append(nbk); bvs.append(nbv)
    y_prompt = rmsnorm(xp, g_final)
    y_sample = rmsnorm(xs, g_final)
    fox_k_p = jnp.stack(fkp); fox_v_p = jnp.stack(fvp); fox_logf_p = jnp.stack(flp)
    band_k_p = jnp.stack(bkp); band_v_p = jnp.stack(bvp)
    mem_k_p = jnp.stack(mkp); mem_v_p = jnp.stack(mvp)
    fox_k_s = jnp.stack(fks); fox_v_s = jnp.stack(fvs); fox_logf_s = jnp.stack(fls)
    band_k_s = jnp.stack(bks); band_v_s = jnp.stack(bvs)
    return (y_prompt, y_sample, fox_k_p, fox_v_p, fox_logf_p, band_k_p, band_v_p, mem_k_p, mem_v_p,
            fox_k_s, fox_v_s, fox_logf_s, band_k_s, band_v_s)


_drawn_inputs = setup_inputs


def setup_inputs(seed=0):
    import zlib

    import numpy as np

    out = dict(_drawn_inputs(seed))
    spreads = {}
    factors = {'cache_fox_logf': 11.389,
     'g_out_band': 3.111,
     'g_cross': 6.256,
     'g_mem': 2.897,
     'b_router1': 21.593,
     'b_router2': 24.742,
     'g_final': 8.449,
     'g_out_fox': 2.932,
     'g_ffn': 6.306}
    for name, (base, spread) in spreads.items():
        noise = np.random.default_rng([zlib.crc32(name.encode()), seed]).standard_normal(out[name].shape)
        drawn = base * np.exp(spread * noise) if base else spread * noise
        out[name] = __import__('jax').numpy.asarray(drawn.astype(out[name].dtype))
    for name, factor in factors.items():
        out[name] = (out[name] * factor).astype(out[name].dtype)
    return out
```

```python
from contextlib import ExitStack

import concourse.bass as bass
from concourse import mybir

F32 = mybir.dt.float32
F32R = mybir.dt.float32r
U32 = mybir.dt.uint32
I32 = mybir.dt.int32
ALU = mybir.AluOpType
ACT = mybir.ActivationFunctionType
AX = mybir.AxisListType

P = 128
D = 1024
C = D // P
NP_TOK, NS_TOK = 256, 64
NTOK = NP_TOK + NS_TOK
TILES = 3
ROWS = [128, 128, 64]
OFF = [0, 128, 256]
HEADS, DH = 8, 64
W = HEADS * DH
M4 = W // P
PAST = 512
PB = PAST // P
CLIP = 128
NMEM, HM = 256, 4
MB = NMEM // P
NG, EPG = 4, 8
NE = NG * EPG
DE = 512
FC = DE // P
SLOTS = 64
ROUNDS = NTOK // SLOTS
RING = 6
EPS = 1e-6
NEG = -1e30
Q_SCALE = DH ** -0.5
MEM_SCALE = 128 ** -0.5

A_GROUP = [0, 43]
A_FL, A_CTOK, A_CPRO, A_CPAST, A_REL = 11, 12, 13, 14, 15
A_PV = [19, 54]
A_WOUT = 78
A_MEM = 84
A_CQ = 90
A_XPV = 94
A_CO = 106
A_ROUTE = 112
A_POS = 113
T_MIX = 0
T_CACHE = [6, 45]
T_KBACK = [10, 49]
T_ATT = [13, 52]
T_MERGE = 84
T_MEM = 90
T_CMK = 94
T_MKBACK = 96
T_CROSS = 98
T_XATT = 104
T_OX = 116
T_FFN = 119
N_MIX, N_MERGE, N_MEM, N_CROSS, N_FFN, N_FINAL = 0, 3, 6, 8, 11, 14


def build(nc, i, o):
    with ExitStack() as ctx:
        def sb(name, shape, dt=F32):
            return ctx.enter_context(nc.sbuf_tensor(name, shape, dt))

        def sem(name):
            return ctx.enter_context(nc.semaphore(name))

        def dram(name, shape, dt=F32):
            return nc.dram_tensor(name, shape, dt, kind="Internal").ap()

        ring = [sb(f"ring{s}", [P, 4096]) for s in range(RING)]
        xres = sb("xres", [P, TILES, D])
        srow = sb("srow", [P, 2, PAST + NS_TOK])
        pT = sb("pT", [P, 2, 5, P])
        zone = sb("zone", [P, 8192])

        kcT = zone[:, 0:2048].rearrange("p (m k) -> p m k", m=M4)
        vc = zone[:, 2048:4096].rearrange("p (b w) -> p b w", b=PB)
        qT = zone[:, 4096:5376].rearrange("p (m t) -> p m t", m=M4)
        kT = zone[:, 5376:6656].rearrange("p (m t) -> p m t", m=M4)
        v = zone[:, 6656:8192].rearrange("p (t w) -> p t w", t=TILES)

        xmem = zone[:, 0:2048].rearrange("p (t d) -> p t d", t=MB)
        mktok = zone[:, 0:1024].rearrange("p (t w) -> p t w", t=MB)
        memT = zone[:, 2048:4096].rearrange("p (c t) -> p c t", c=C)
        cmv = zone[:, 4096:5120].rearrange("p (b w) -> p b w", b=MB)
        cmkT = zone[:, 5120:6144].rearrange("p (m k) -> p m k", m=HM)
        mkT = zone[:, 6144:7168].rearrange("p (m k) -> p m k", m=HM)
        mv = zone[:, 7168:8192].rearrange("p (b w) -> p b w", b=MB)

        xg = zone[0:SLOTS, 0:2048].rearrange("p (b d) -> p b d", b=2)
        xeT = zone[:, 2048:3072].rearrange("p (b c s) -> p b c s", b=2, c=C)
        aT = zone[:, 3072:3584].rearrange("p (b f) -> p b f", b=2)
        sg = zone[:, 3584:4096].rearrange("p (b f) -> p b f", b=2)
        ysb = zone[0:SLOTS, 4096:6144].rearrange("p (b d) -> p b d", b=2)
        ygat = zone[:, 0:6144].rearrange("p (t k d) -> p t k d", t=TILES, k=2)
        gfin = zone[:, 6144:7168]

        ident = sb("ident", [P, P])
        anti = sb("anti", [P, P])
        tri = sb("tri", [P, P])
        stri = sb("stri", [P, P])
        ones = sb("ones", [P, P])
        cmask = sb("cmask", [P, 256])
        mhalf = sb("mhalf", [P, 2])
        iota32 = sb("iota32", [P, NE])
        tokid = sb("tokid", [P, TILES], U32)
        zero_u = sb("zero_u", [P, NTOK * NE // P], U32)
        gcol = sb("gcol", [P, 5, C])
        bfb = sb("bfb", [P, HEADS])
        wfl = sb("wfl", [P, C, HEADS])
        wr = sb("wr", [P, C, NG + NE])
        brb = sb("brb", [P, NG + NE])
        relT = pT[0:HEADS, 1, 0:3, :].rearrange("p b q -> p (b q)")
        t256 = sb("t256", [NS_TOK, HEADS])
        ss = sb("ss", [P, 2 * 17])
        ms = sb("ms", [P, 2 * 17])
        rstd = sb("rstd", [P, 2 * 17])
        flx = sb("flx", [P, 24])
        flz = sb("flz", [P, 24])
        fla = sb("fla", [P, 24])
        lfb = sb("lfb", [P, TILES, HEADS])
        clf = sb("clf", [P, PB, HEADS])
        cq = sb("cq", [P, 24])
        ckT = sb("ckT", [P, NP_TOK + PAST + NS_TOK])
        negmax = sb("negmax", [P, 2])
        rowsum = sb("rowsum", [P, 2])
        rinv = sb("rinv", [P, 2])
        route = pT[:, 0, :, :].rearrange("p b q -> p (b q)")
        lg = sb("lg", [P, TILES, NG + NE])
        lg8 = sb("lg8", [P, TILES, 8])
        top1 = sb("top1", [P, TILES, 8])
        top1i = sb("top1i", [P, TILES, 8], U32)
        nm1 = sb("nm1", [P, TILES])
        ex4 = sb("ex4", [P, TILES, NG])
        s4 = sb("s4", [P, TILES])
        gidx = sb("gidx", [P, TILES])
        goh = sb("goh", [P, TILES, NG])
        l2m = route[:, 0:96].rearrange("p (t g e) -> p t g e", t=TILES, g=NG)
        l2g = sb("l2g", [P, TILES, EPG])
        top2 = sb("top2", [P, TILES, 8])
        top2i = sb("top2i", [P, TILES, 8], U32)
        dlt = sb("dlt", [P, TILES])
        edl = sb("edl", [P, TILES])
        gate = sb("gate", [P, 2, TILES])
        eid = sb("eid", [P, 2, TILES])
        moh = route[:, 96:288].rearrange("p (k t e) -> p k t e", k=2, t=TILES)
        mboth = route[:, 288:384].rearrange("p (t e) -> p t e", t=TILES)
        posb = sb("posb", [P, TILES, NE])
        keyb = route[:, 384:480].rearrange("p (t e) -> p t e", t=TILES)
        kprod = route[:, 480:576].rearrange("p (t e) -> p t e", t=TILES)
        keyf = sb("keyf", [P, 2, TILES])
        slot = sb("slot", [P, 2, TILES], U32)
        cnt = sb("cnt", [P, 1])
        cnti = sb("cnti", [P, 1], I32)
        idx_all = srow[0:SLOTS, 0, 0:ROUNDS * NE + 1].bitcast(U32)
        idx_cur = [sb(f"idx_cur{b}", [SLOTS, 1], U32) for b in range(2)]

        with ExitStack() as front:
            def fsb(name, shape):
                return front.enter_context(nc.sbuf_tensor(name, shape, F32))

            hT = fsb("hT", [P, C, NTOK])
            hn = fsb("hn", [P, 2, D])
            oall = fsb("oall", [P, TILES, D])
            ktok = fsb("ktok", [P, TILES, W])
            relb = fsb("relb", [P, HEADS, 256])
        stage = hn[:, :, :].rearrange("p a (b w) -> p (a b) w", w=W)
        hankel = oall[:, 0:2, :].rearrange("p t (h j) -> p (t h) j", j=256)
        qxT = relb[:, :, :].rearrange("p h k -> p (h k)")[:, 0:M4 * NTOK].rearrange("p (m t) -> p m t", m=M4)
        w_hi = sb("w_hi", [P, FC, D], F32R)
        w_lo = sb("w_lo", [P, FC, D], F32R)
        a_split = sb("a_split", [P, 2, FC, 2, SLOTS], F32R)

        pA = [ctx.enter_context(nc.psum_tensor(f"pA{b}", [P, 512], F32)) for b in range(2)]
        pTr = [ctx.enter_context(nc.psum_tensor(f"pTr{b}", [P, 512], F32)) for b in range(2)]
        pS = [ctx.enter_context(nc.psum_tensor(f"pS{b}", [P, 1024], F32)) for b in range(2)]

        relT_d = dram("relT_d", [HEADS, 384])
        hn_d = dram("hn_d", [NTOK, D])
        slot_d = dram("slot_d", [NTOK * NE, 1], U32)
        y_d = dram("y_d", [NTOK * NE, D])

        x_in = [sem(f"x_in{t}") for t in range(TILES)]
        gmix_in = sem("gmix_in")
        small_in = sem("small_in")
        rel_raw = sem("rel_raw")
        rel_rows = sem("rel_rows")
        rel_stored = sem("rel_stored")
        rel_in = sem("rel_in")
        rel_ready = sem("rel_ready")
        clf_in = sem("clf_in")
        stage_in = [sem(f"stage_in{g}") for g in range(2)]
        vc_in = [sem(f"vc_in{g}") for g in range(2)]
        xmem_in = sem("xmem_in")
        cmk_in = sem("cmk_in")
        cmv_in = sem("cmv_in")
        gfin_in = sem("gfin_in")
        w_in_s = [sem(f"w_loaded{s}") for s in range(RING)]
        gate_read = sem("gate_read")
        pe_passed = sem("pe_passed")
        pool_passed = sem("pool_passed")
        consts = sem("consts")
        pool_step = sem("pool_step")
        dve_step = sem("dve_step")
        act_step = sem("act_step")
        sq_done = sem("sq_done")
        rstd_done = sem("rstd_done")
        hn_ready = sem("hn_ready")
        hn_stored = [sem(f"hn_stored{t}") for t in range(TILES)]
        a_ready = sem("a_ready")
        a_used = sem("a_used")
        t_ready = sem("t_ready")
        t_used = sem("t_used")
        z_ready = sem("z_ready")
        ln_ready = sem("ln_ready")
        lf_ready = sem("lf_ready")
        sc_ready = sem("sc_ready")
        sc_used = sem("sc_used")
        max_ready = sem("max_ready")
        exp_done = sem("exp_done")
        rinv_done = sem("rinv_done")
        ktok_stored = [sem(f"ktok_stored{t}") for t in range(TILES)]
        v_stored = sem("v_stored")
        mk_stored = sem("mk_stored")
        out_stored = sem("out_stored")
        top1_ready = sem("top1_ready")
        ex4_ready = sem("ex4_ready")
        dlt_ready = sem("dlt_ready")
        edl_ready = sem("edl_ready")
        moh_ready = sem("moh_ready")
        slot_ready = sem("slot_ready")
        slot_zeroed = sem("slot_zeroed")
        slot_stored = sem("slot_stored")
        idx_in = sem("idx_in")
        idx_copied = sem("idx_copied")
        xg_in = [sem(f"xg_in{b}") for b in range(2)]
        xt_ready = sem("xt_ready")
        xe_ready = sem("xe_ready")
        gu_ready = sem("gu_ready")
        sig_ready = sem("sig_ready")
        at_ready = sem("at_ready")
        y_ready = sem("y_ready")
        w_hi_ready = sem("w_hi_ready")
        w_lo_ready = sem("w_lo_ready")
        a_split_step = sem("a_split_step")
        y_lower = sem("y_lower")
        y_summed = sem("y_summed")
        y_stored = [sem(f"y_stored{b}") for b in range(2)]
        moe_done = sem("moe_done")
        other_stored = sem("other_stored")
        yg_in = [sem(f"yg_in{t}") for t in range(TILES)]
        xfin_ready = sem("xfin_ready")
        yout_ready = sem("yout_ready")

        xp_d = i["x_prompt"][0].rearrange("(t p) d -> p t d", p=P)
        xs_d = i["x_sample"][0]
        w_in = i["w_in"][0].rearrange("(p c) n -> p c n", c=C)
        w_out = i["w_out"][0].rearrange("(p c) n -> p c n", c=C)
        flat = "t h d -> t (h d)"
        cache_k = [i["cache_fox_k"][0, 0].rearrange(flat), i["cache_band_k"][0, 0].rearrange(flat)]
        cache_v = [i["cache_fox_v"][0, 0].rearrange(flat), i["cache_band_v"][0, 0].rearrange(flat)]
        k_p = [o["fox_k_p"][0, 0].rearrange(flat), o["band_k_p"][0, 0].rearrange(flat)]
        v_p = [o["fox_v_p"][0, 0].rearrange(flat), o["band_v_p"][0, 0].rearrange(flat)]
        new = PAST - NS_TOK
        k_s = [o["fox_k_s"][0, 0].rearrange(flat), o["band_k_s"][0, 0].rearrange(flat)[new:, :]]
        v_s = [o["fox_v_s"][0, 0].rearrange(flat), o["band_v_s"][0, 0].rearrange(flat)[new:, :]]

        def cols(w, n):
            return w[:, :, n * 512:(n + 1) * 512]

        front_weights = [cols(w_in, 0), cols(w_in, 1), cols(w_in, 2), cols(w_in, 3), cols(w_in, 4), cols(w_in, 5),
                         cols(w_out, 0), cols(w_out, 1),
                         i["w_ck"][0].rearrange("(p c) n -> p c n", c=C),
                         i["w_cv"][0].rearrange("(p c) n -> p c n", c=C),
                         i["w_cq"][0].rearrange("(p c) n -> p c n", c=C),
                         i["w_co"][0].rearrange("(c p) n -> p c n", p=P)]
        assert len(front_weights) == 2 * RING
        a_done = [4, 8, 11, A_GROUP[1] + 4, A_GROUP[1] + 8, A_GROUP[1] + 11, A_WOUT + 6, A_WOUT + 6,
                  A_MEM + HM, A_MEM + HM + MB, A_CQ + M4, A_CO + 6]
        J_Q, J_K, J_V, J_WOUT, J_CK, J_CV, J_CQ, J_CO = 0, 1, 2, 6, 8, 9, 10, 11

        def by_k(j, k=C):
            return ring[j % RING][:, :].rearrange("p (c n) -> p c n", c=k)

        t_of = [T_MIX + 2 * t for t in range(3)] + [T_MERGE + 2 * t for t in range(3)] + [T_MEM, T_MEM + 2] \
            + [T_CROSS + 2 * t for t in range(3)] + [T_FFN + 2 * t for t in range(3)]

        def units(g):
            if g < 2:
                return [(h, t, [128, 256, PAST + NS_TOK][t]) for h in range(HEADS) for t in range(TILES)]
            return [(h, t, NMEM) for h in range(HM) for t in range(TILES)]

        block = ctx.enter_context(nc.Block())

        @block.sync
        def _(sp):
            def load_weights(j):
                if j >= RING:
                    sp.wait_ge(a_ready, a_done[j - RING])
                sp.dma_start(by_k(j, front_weights[j].shape[1]), front_weights[j]).then_inc(w_in_s[j % RING], 16)

            for t in range(2):
                sp.dma_start(xres[:, t, :], xp_d[:, t, :]).then_inc(x_in[t], 16)
            sp.dma_start(xres[0:NS_TOK, 2, :], xs_d).then_inc(x_in[2], 16)
            load_weights(0)
            load_weights(1)
            small = 0
            for dst, src in ((gcol[0:64, 1, :], i["g_out_fox"][0].rearrange("(p c) -> p c", c=C)),
                             (gcol[64:128, 1, :], i["g_out_band"][0].rearrange("(p c) -> p c", c=C)),
                             (gcol[:, 2, :], i["g_mem"][0].rearrange("(p c) -> p c", c=C)),
                             (gcol[:, 3, :], i["g_cross"][0].rearrange("(p c) -> p c", c=C)),
                             (gcol[:, 4, :], i["g_ffn"][0].rearrange("(p c) -> p c", c=C)),
                             (wfl[:, :, :], w_in[:, :, 6 * W:6 * W + HEADS]),
                             (bfb[:, :], i["b_forget"][0].partition_broadcast(P)),
                             (t256[:, :], i["rel_table"][0, 2 * CLIP].partition_broadcast(NS_TOK)),
                             (wr[:, :, 0:NG], i["w_router1"][0].rearrange("(p c) n -> p c n", c=C)),
                             (wr[:, :, NG:], i["w_router2"][0].rearrange("(p c) n -> p c n", c=C)),
                             (brb[:, 0:NG], i["b_router1"][0].partition_broadcast(P)),
                             (brb[:, NG:], i["b_router2"][0].partition_broadcast(P)),
                             (clf[:, :, :], i["cache_fox_logf"][0, 0].rearrange("(b p) h -> p b h", p=P))):
                sp.dma_start(dst, src).then_inc(small_in, 16)
                small += 16
            assert small == SMALL
            table = i["rel_table"][0]
            with nc.allow_non_contiguous_dma(reason="the table by heads"):
                sp.dma_start(relT[:, 0:2 * CLIP + 1], table.rearrange("r h -> h r")).then_inc(rel_raw, 16)
            load_weights(2)
            sp.wait_ge(t_ready, T_MIX + 6)
            sp.dma_start(stage, cache_k[0].rearrange("(b p) w -> p b w", p=P)).then_inc(stage_in[0], 16)
            sp.dma_start(vc, cache_v[0].rearrange("(b p) w -> p b w", p=P)).then_inc(vc_in[0], 16)
            load_weights(3)
            load_weights(4)
            load_weights(5)
            sp.wait_ge(t_ready, T_CACHE[0] + 4)
            sp.dma_start(stage, cache_k[1].rearrange("(b p) w -> p b w", p=P)).then_inc(stage_in[1], 16)
            load_weights(6)
            load_weights(7)
            load_weights(8)
            sp.wait_ge(a_ready, A_PV[0] + 24)
            sp.dma_start(vc, cache_v[1].rearrange("(b p) w -> p b w", p=P)).then_inc(vc_in[1], 16)
            load_weights(9)
            load_weights(10)
            load_weights(11)
            sp.wait_ge(a_ready, A_PV[1] + 24)
            sp.dma_start(xmem, i["mem_prompt"][0].rearrange("(t p) d -> p t d", p=P)).then_inc(xmem_in, 16)
            sp.dma_start(cmv, i["cache_mem_v"][0, 0].rearrange("(b p) h d -> p b (h d)", p=P)).then_inc(cmv_in, 16)
            for t in range(TILES):
                sp.wait_ge(ktok_stored[t], 32)
            sp.dma_start(ktok[:, 0:MB, :], i["cache_mem_k"][0, 0].rearrange("(b p) h d -> p b (h d)", p=P)).then_inc(cmk_in, 16)

            def pair(r, p, first=False):
                for b in range(2):
                    e = p * 2 + b
                    for n, name in enumerate(("w_exp_gate", "w_exp_up", "w_exp_down")):
                        s = 3 * b + n
                        if first:
                            sp.wait_ge(a_ready, a_done[RING + s])
                        elif n < 2:
                            sp.wait_ge((gate_read, gu_ready)[n], r * NE + e - 1)
                        else:
                            sp.wait_ge(w_lo_ready, (r * NE + e - 1) * FC)
                        if isinstance(e, int):
                            src = i[name][0, e]
                        else:
                            src = i[name][0, bass.ds(e, 1)].rearrange("a k n -> (a k) n")
                        if n < 2:
                            dst, src = by_k(s), src.rearrange("(p c) n -> p c n", c=C)
                        else:
                            dst, src = by_k(s, FC), src.rearrange("(c p) n -> p c n", p=P)
                        sp.dma_start(dst, src).then_inc(w_in_s[s], 16)

            pair(0, 0, True)
            with sp.Fori(1, NE // 2) as p:
                pair(0, p)
            sp.wait_ge(slot_ready, 1)
            most = sp.value_load(cnti[0:1, 0:1], min_val=0, max_val=NTOK)
            with sp.If(most > SLOTS):
                with sp.Fori(1, ROUNDS) as r:
                    with sp.Fori(0, NE // 2) as p:
                        pair(r, p)
            sp.wait_ge(moe_done, 1)
            sp.dma_start(gfin, i["g_final"].partition_broadcast(P)).then_inc(gfin_in, 16)
            for t in range(TILES):
                sp.wait_ge(yout_ready, t + 1)
                dst = o["y_prompt"][0, t * P:(t + 1) * P, :] if t < 2 else o["y_sample"][0]
                sp.dma_start(dst, oall[0:ROWS[t], t, :]).then_inc(out_stored, 16)
            sp.wait_ge(out_stored, 16 * TILES)

        @block.gpsimd
        def _(pool):
            steps = [0]

            def step(ins):
                steps[0] += 1
                ins.then_inc(pool_step, 1)
                pool.wait_ge(pool_step, steps[0])

            pool.memset(ident[:, :], 0.0)
            pool.memset(anti[:, :], 0.0)
            pool.memset(ones[:, :], 1.0)
            pool.memset(cmask[:, :], 0.0)
            pool.memset(mhalf[:, :], -0.5)
            step(pool.memset(zero_u[:, :], 0))
            pool.dma_start(slot_d.rearrange("(p n) a -> p (n a)", p=P), zero_u[:, :]).then_inc(slot_zeroed, 16)
            pool.affine_select(out=ident[:, :], in_=ident[:, :], compare_op=ALU.not_equal, fill=1.0, base=0,
                               pattern=[[-1, P]], channel_multiplier=1)
            pool.affine_select(out=anti[:, :], in_=anti[:, :], compare_op=ALU.not_equal, fill=1.0, base=1 - P,
                               pattern=[[1, P]], channel_multiplier=1)
            pool.affine_select(out=tri[:, :], in_=ones[:, :], compare_op=ALU.is_ge, fill=0.0, base=0,
                               pattern=[[1, P]], channel_multiplier=-1)
            pool.affine_select(out=stri[:, :], in_=ones[:, :], compare_op=ALU.is_ge, fill=0.0, base=-1,
                               pattern=[[1, P]], channel_multiplier=-1)
            pool.affine_select(out=cmask[:, :], in_=cmask[:, :], compare_op=ALU.is_ge, fill=NEG, base=P,
                               pattern=[[-1, 256]], channel_multiplier=1)
            pool.iota(tokid[:, :], pattern=[[P, TILES]], base=0, channel_multiplier=1)
            pool.iota(iota32[:, :], pattern=[[1, NE]], base=0, channel_multiplier=0,
                      allow_small_or_imprecise_dtypes=True).then_inc(consts, 1)

            def rsqrt(n, two=False, width=D):
                rows = slice(0, unit_rows(n))
                cs = slice(2 * n, 2 * n + (2 if two else 1))
                pool.wait_ge(sq_done, n + 1)
                step(pool.tensor_scalar(ms[rows, cs], ss[rows, cs], 1.0 / width, EPS, ALU.mult, ALU.add))
                pool.tensor_tensor(rstd[rows, cs], ms[rows, cs], mhalf[rows, 0:2 if two else 1],
                                   ALU.pow).then_inc(rstd_done, 1)

            stores = [0]

            def store(dst, src, s=None, wait=None):
                if s is None:
                    stores[0] += 1
                pool.dma_start(dst, src).then_inc(s if s is not None else other_stored, 16)

            for n in range(N_MIX, N_MIX + 3):
                rsqrt(n)
            pool.wait_ge(rel_rows, 1)
            pool.dma_start(relT_d, relT).then_inc(rel_stored, 16)
            pool.wait_ge(rel_stored, 16)
            rows = bass.AP(tensor=relT_d.tensor, offset=1, ap=[[1, P], [384, HEADS], [1, 256]])
            pool.dma_start(hankel, rows).then_inc(rel_in, 16)
            store(o["band_k_s"][0, 0].rearrange(flat)[0:new, :], cache_k[1][NS_TOK:, :])
            store(o["band_v_s"][0, 0].rearrange(flat)[0:new, :], cache_v[1][NS_TOK:, :])
            for g in range(2):
                if g == 1:
                    pool.wait_ge(a_used, A_REL + 4)
                    pool.memset(relb[0:64, :, 192:256], NEG).then_inc(rel_ready, 1)
                for t in range(TILES):
                    pool.wait_ge(t_used, T_KBACK[g] + t + 1)
                    dst = k_p[g][t * P:(t + 1) * P, :] if t < 2 else k_s[g]
                    store(dst, ktok[0:ROWS[t], t, :], ktok_stored[t])
                pool.wait_ge(a_used, A_GROUP[g] + 11)
                store(v_p[g].rearrange("(t p) w -> p t w", p=P), v[:, 0:2, :], v_stored)
                store(v_s[g], v[0:NS_TOK, 2, :], v_stored)
                if g == 0:
                    pool.wait_ge(lf_ready, 1)
                    store(o["fox_logf_p"][0, 0].rearrange("(t p) h -> p t h", p=P), lfb[:, 0:2, :])
                    store(o["fox_logf_s"][0, 0], lfb[0:NS_TOK, 2, :])
            for n in range(N_MERGE, N_MERGE + 3):
                rsqrt(n, True, W)
            for n in range(N_MEM, N_MEM + 2):
                rsqrt(n)
            for n in range(N_CROSS, N_CROSS + 3):
                rsqrt(n)
            pool.wait_ge(t_used, T_MKBACK + 2)
            store(o["mem_k_p"][0, 0].rearrange("(b p) h d -> p b (h d)", p=P), mktok, mk_stored)
            pool.wait_ge(a_used, A_MEM + 6)
            store(o["mem_v_p"][0, 0].rearrange("(b p) h d -> p b (h d)", p=P), mv, mk_stored)
            for t in range(TILES):
                rsqrt(N_FFN + t)
                pool.wait_ge(hn_ready, N_FFN + t + 1)
                store(hn_d[OFF[t]:OFF[t] + ROWS[t], :], hn[0:ROWS[t], (N_FFN + t) % 2, :], hn_stored[t])

            step(pool.memset(idx_all[:, ROUNDS * NE:], 0))
            pool.wait_ge(slot_ready, 1)
            pool.wait_ge(slot_zeroed, 16)
            for t in range(TILES):
                for k in range(2):
                    pool.indirect_dma_start(
                        out=slot_d, out_offset=bass.IndirectOffsetOnAxis(ap=slot[0:ROWS[t], k, t:t + 1], axis=0),
                        in_=tokid[0:ROWS[t], t:t + 1], in_offset=None).then_inc(slot_stored, 16)
            pool.wait_ge(slot_stored, 16 * 2 * TILES)
            pool.dma_start(idx_all[:, 0:ROUNDS * NE].rearrange("p (r e) -> p r e", r=ROUNDS),
                           slot_d.rearrange("(r p e) a -> p r (e a)", p=SLOTS, e=NE)).then_inc(idx_in, 16)
            pool.wait_ge(idx_in, 16)
            for t in range(TILES):
                pool.wait_ge(hn_stored[t], 16)
            pool.wait_ge(mk_stored, 32)

            def gather(n, b, first=False):
                if not first:
                    pool.wait_ge(xt_ready, n - 1)
                col = idx_all[:, n:n + 1] if isinstance(n, int) else idx_all[:, bass.ds(n, 1)]
                pool.tensor_copy(idx_cur[b][:, :], col).then_inc(idx_copied, 1)
                pool.wait_ge(idx_copied, n + 1)
                pool.nop().then_inc(pool_passed, 1)
                pool.indirect_dma_start(out=xg[:, b, :], out_offset=None, in_=hn_d,
                                        in_offset=bass.IndirectOffsetOnAxis(ap=idx_cur[b][:, :], axis=0)).then_inc(xg_in[b], 16)

            def take_rows(table, experts):
                pool.wait_ge(moe_done, 1)
                pool.wait_ge(xe_ready, experts + 1)
                for t in range(TILES):
                    for k in range(2):
                        pool.indirect_dma_start(out=ygat[0:ROWS[t], t, k, :], out_offset=None, in_=table,
                                                in_offset=bass.IndirectOffsetOnAxis(ap=slot[0:ROWS[t], k, t:t + 1], axis=0)).then_inc(yg_in[t], 16)

            gather(0, 0, True)
            gather(1, 1, True)
            gather(2, 0)
            with pool.Fori(1, NE // 2) as p:
                gather(p * 2 + 1, 1)
                gather(p * 2 + 2, 0)
            most = pool.value_load(cnti[0:1, 0:1], min_val=0, max_val=NTOK)
            with pool.If(most > SLOTS):
                with pool.Fori(NE // 2, ROUNDS * NE // 2) as p:
                    gather(p * 2 + 1, 1)
                    gather(p * 2 + 2, 0)
                take_rows(y_d, ROUNDS * NE)
            with pool.Else():
                take_rows(y_d[0:SLOTS * NE, :], NE)
            for t in range(TILES):
                rsqrt(N_FINAL + t)
            pool.wait_ge(other_stored, 16 * stores[0])
            pool.wait_ge(v_stored, 64)
            pool.wait_ge(mk_stored, 32)
            for t in range(TILES):
                pool.wait_ge(ktok_stored[t], 32)

        @block.scalar
        def _(act):
            act.dma_start(gcol[:, 0, :], i["g_mix"][0].rearrange("(p c) -> p c", c=C)).then_inc(gmix_in, 16)

            def norm(n, parts, before=None):
                rows = unit_rows(n)
                dst = hn[0:rows, n % 2, :]
                if n >= 2:
                    act.wait_ge(t_ready, t_of[n - 2] + 2)
                for k, (src, lo, hi) in enumerate(parts):
                    last = act.activation(dst[:, lo:hi], src, ACT.Square, accum_out=ss[0:rows, 2 * n + k:2 * n + k + 1])
                last.then_inc(sq_done, 1)
                act.wait_ge(rstd_done, n + 1)
                for k, (src, lo, hi) in enumerate(parts):
                    last = act.activation(dst[:, lo:hi], src, ACT.Copy, scale=rstd[0:rows, 2 * n + k:2 * n + k + 1])
                last.then_inc(hn_ready, 1)

            def evacuate(j, dst, src, scale=1.0, last=True):
                act.wait_ge(a_ready, j + 1)
                ins = act.activation(dst, src, ACT.Copy, scale=scale)
                if last:
                    ins.then_inc(a_used, 1)

            for t in range(TILES):
                act.wait_ge(x_in[t], 16)
                norm(N_MIX + t, [(xres[0:ROWS[t], t, :], 0, D)])

            def softmax_unit(g, u, n):
                h, t, keys = units(g)[u]
                act.wait_ge(max_ready, n + 1)
                act.activation(srow[0:ROWS[t], n % 2, 0:keys], srow[0:ROWS[t], n % 2, 0:keys], ACT.Exp,
                               bias=negmax[0:ROWS[t], n % 2:n % 2 + 1],
                               accum_out=rowsum[0:ROWS[t], n % 2:n % 2 + 1]).then_inc(exp_done, 1)

            def output_unit(g, u, n, j):
                h, t, _ = units(g)[u]
                rows, dh = ROWS[t], (DH if g < 2 else 128)
                col = (W if g == 1 else 0) + h * dh
                act.wait_ge(rinv_done, n + 1)
                evacuate(j, oall[0:rows, t, col:col + dh], pA[j % 2][0:rows, 0:dh], rinv[0:rows, n % 2:n % 2 + 1])

            def attention(g, n0, j0):
                k = len(units(g))
                for s in range(k + 2):
                    if s < k:
                        softmax_unit(g, s, n0 + s)
                    if s >= 2:
                        output_unit(g, s - 2, n0 + s - 2, j0 + s - 2)

            for g in range(2):
                j = A_GROUP[g]
                for m in range(M4):
                    evacuate(j + m, qT[:, m, :], pA[(j + m) % 2][:, 0:NTOK], Q_SCALE)
                for m in range(M4):
                    evacuate(j + 4 + m, kT[:, m, :], pA[(j + 4 + m) % 2][:, 0:NTOK])
                if g == 1:
                    act.wait_ge(v_stored, 32)
                for t in range(TILES):
                    evacuate(j + 8 + t, v[0:ROWS[t], t, :], pA[(j + 8 + t) % 2][0:ROWS[t], :])
                if g == 0:
                    act.wait_ge(consts, 2)
                    evacuate(A_FL, flx[:, 0:16], pA[A_FL % 2][:, 0:16], last=False)
                    evacuate(A_FL, flx[0:64, 16:24], pA[A_FL % 2][0:64, 16:24])
                    act.wait_ge(z_ready, 1)
                    act.activation(fla[:, :], fla[:, :], ACT.Exp).then_inc(act_step, 1)
                    act.wait_ge(act_step, 1)
                    act.activation(fla[:, :], fla[:, :], ACT.Ln, bias=1.0).then_inc(ln_ready, 1)
                    evacuate(A_CTOK, cq[:, 0:16], pA[A_CTOK % 2][:, 0:16], last=False)
                    evacuate(A_CTOK, cq[0:64, 16:24], pA[A_CTOK % 2][0:64, 16:24])
                    own = NP_TOK + PAST
                    for p0 in (0, 64):
                        b = pA[A_CPRO % 2]
                        evacuate(A_CPRO, ckT[p0:p0 + 8, 0:NP_TOK], b[0:8, 0:NP_TOK], -1.0, last=False)
                        evacuate(A_CPRO, ckT[p0:p0 + 8, own:own + NS_TOK], b[0:8, NP_TOK:NTOK], -1.0, last=p0 > 0)
                    for p0 in (0, 64):
                        evacuate(A_CPAST, ckT[p0:p0 + 8, NP_TOK:own], pA[A_CPAST % 2][0:8, :], -1.0, last=p0 > 0)
                    for x in range(4):
                        evacuate(A_REL + x, relb[:, 2 * x:2 * x + 2, :], pA[(A_REL + x) % 2][:, :].rearrange("p (h k) -> p h k", h=2))
                attention(g, 24 * g, A_PV[g])

            act.wait_ge(a_used, A_WOUT)
            for t in range(TILES):
                o_t = oall[0:ROWS[t], t, :]
                norm(N_MERGE + t, [(o_t[:, 0:W], 0, W), (o_t[:, W:], W, D)])
            act.wait_ge(xmem_in, 16)
            for t in range(MB):
                norm(N_MEM + t, [(xmem[:, t, :], 0, D)])

            def cross_norm(t):
                act.wait_ge(a_used, A_WOUT + 2 * t + 2)
                norm(N_CROSS + t, [(xres[0:ROWS[t], t, :], 0, D)])

            cross_norm(0)
            cross_norm(1)
            act.wait_ge(v_stored, 64)
            for m in range(HM):
                evacuate(A_MEM + m, mkT[:, m, :], pA[(A_MEM + m) % 2][:, 0:NMEM])
            for b in range(MB):
                evacuate(A_MEM + HM + b, mv[:, b, :], pA[(A_MEM + HM + b) % 2][:, :])
            cross_norm(2)
            for m in range(M4):
                evacuate(A_CQ + m, qxT[:, m, :], pA[(A_CQ + m) % 2][:, 0:NTOK])
            attention(2, 48, A_XPV)
            for t in range(TILES):
                if t == 2:
                    act.wait_ge(hn_stored[0], 16)
                act.wait_ge(a_used, A_CO + 2 * t + 2)
                norm(N_FFN + t, [(xres[0:ROWS[t], t, :], 0, D)])
            act.wait_ge(top1_ready, 1)
            for t in range(TILES):
                ins = act.activation(ex4[:, t, :], lg[:, t, 0:NG], ACT.Exp, bias=nm1[:, t:t + 1], accum_out=s4[:, t:t + 1])
            ins.then_inc(ex4_ready, 1)
            act.wait_ge(dlt_ready, 1)
            act.activation(edl[:, :], dlt[:, :], ACT.Exp).then_inc(edl_ready, 1)

            def split(b, chunks):
                for f in chunks:
                    act.activation(w_hi[:, f, :], by_k(3 * b + 2, FC)[:, f, :], ACT.Copy).then_inc(w_hi_ready, 1)

            def sigmoid(n, b, first=False):
                act.wait_ge(gu_ready, n + 1)
                if not first:
                    act.wait_ge(at_ready, n - 1)
                act.activation(sg[:, b, :], pA[b][:, 0:256], ACT.Sigmoid).then_inc(sig_ready, 1)

            def lower_rows(n, b, first=False):
                act.wait_ge(y_ready, n + 1)
                if not first:
                    act.wait_ge(y_stored[b], (n - b) * 8)
                act.activation(ysb[:, b, :], pS[b][SLOTS:, :], ACT.Copy).then_inc(y_lower, 1)

            def rows_out(n, b, r, e):
                act.wait_ge(y_summed, n + 1)
                at_r = r if isinstance(r, int) else bass.ds(r, 1)
                at_e = e if isinstance(e, int) else bass.ds(e, 1)
                dst = y_d.rearrange("(r p e) d -> r e p d", p=SLOTS, e=NE)[at_r, at_e]
                if len(dst.shape) == 4:
                    dst = dst.rearrange("a b p d -> (a b p) d")
                elif len(dst.shape) == 3:
                    dst = dst.rearrange("a p d -> (a p) d")
                act.dma_start(dst, ysb[:, b, :]).then_inc(y_stored[b], 16)

            def expert(r, e, b, first=False, first_out=False):
                n = r * NE + e
                sigmoid(n, b, first)
                lower_rows(n - 1, 1 - b, first_out)
                act.wait_ge(w_in_s[3 * b + 2], (n - b) * 8 + 48)
                split(b, (0,))
                rows_out(n - 1, 1 - b, r, e - 1)
                split(b, range(1, FC))

            def experts(r):
                n = r * NE
                act.wait_ge(w_in_s[2], n * 8 + 48)
                split(0, range(FC))
                first = isinstance(r, int)
                sigmoid(n, 0, first)
                expert(r, 1, 1, first, first)
                expert(r, 2, 0, False, first)
                expert(r, 3, 1)
                with act.Fori(2, NE // 2) as p:
                    for b in range(2):
                        expert(r, p * 2 + b, b)
                lower_rows(n + NE - 1, 1)
                rows_out(n + NE - 1, 1, r, NE - 1)

            act.wait_ge(a_ready, A_ROUTE + 1)
            for t in range(TILES):
                act.wait_ge(hn_stored[t], 16)
            experts(0)
            for b in range(2):
                act.wait_ge(y_stored[b], 16 * (NE // 2))
            most = act.value_load(cnti[0:1, 0:1], min_val=0, max_val=NTOK)
            with act.If(most > SLOTS):
                with act.Fori(1, ROUNDS) as r:
                    experts(r)
                for b in range(2):
                    act.wait_ge(y_stored[b], 16 * (ROUNDS * NE // 2))
            act.activation(sg[:, 0, 0:1], ones[:, 0:1], ACT.Copy).then_inc(moe_done, 1)
            for t in range(TILES):
                rows, n = ROWS[t], N_FINAL + t
                act.wait_ge(xfin_ready, t + 1)
                act.activation(oall[0:rows, t, :], xres[0:rows, t, :], ACT.Square,
                               accum_out=ss[0:rows, 2 * n:2 * n + 1]).then_inc(sq_done, 1)

        @block.tensor
        def _(pe):
            mm = nc.tensor.matmul

            def a_bank(j):
                if j >= 2:
                    pe.wait_ge(a_used, j - 1)
                return pA[j % 2]

            def t_bank(j):
                if j >= 2:
                    pe.wait_ge(t_used, j - 1)
                return pTr[j % 2]

            def weights(j):
                pe.wait_ge(w_in_s[j % RING], 16 * (j // RING + 1))
                return by_k(j, front_weights[j].shape[1])

            def transpose_norm(n, j, rows):
                pe.wait_ge(hn_ready, n + 1)
                src = hn[0:rows, n % 2, :].rearrange("t (p c) -> t c p", c=C)
                for half in range(2):
                    bank = t_bank(j + half)
                    for c in range(4):
                        last = nc.tensor.transpose(bank[:, c * P:c * P + rows], src[:, 4 * half + c, :], ident[0:rows, 0:rows])
                    if half == 0:
                        last.then_inc(t_ready, 1)
                last.then_inc(t_ready, 1)

            def by_weights(j, w, xT, n, m):
                bank = a_bank(j)
                for c in range(C):
                    last = mm(bank[:, 0:n], w[:, c, m * P:(m + 1) * P], xT[:, c, 0:n], start=c == 0, stop=c == C - 1)
                last.then_inc(a_ready, 1)
                return last

            def by_tokens(j, lhs, w, k, cols_, rows):
                bank = a_bank(j)
                for c in range(k):
                    last = mm(bank[0:rows, 0:512], lhs(c), w[:, c, cols_], start=c == 0, stop=c == k - 1)
                last.then_inc(a_ready, 1)

            pe.wait_ge(consts, 1)
            for t in range(TILES):
                transpose_norm(N_MIX + t, T_MIX + 2 * t, ROWS[t])
            pe.wait_ge(t_used, T_CACHE[0])

            def attention(g, n0, j0, t0):
                us = units(g)
                tj = [t0]
                ready_at = {}

                def scores(u):
                    h, t, keys = us[u]
                    n = n0 + u
                    rows, q0 = ROWS[t], OFF[t]
                    if n >= 2:
                        pe.wait_ge(sc_used, n - 1)
                    bank = pS[n % 2]
                    if g == 2:
                        kk = mkT if t < 2 else cmkT
                        mm(bank[0:rows, 0:keys], qxT[:, h, q0:q0 + rows], kk[:, h, :], start=True, stop=True).then_inc(sc_ready, 1)
                        return
                    p0, m = 64 * (h % 2), h // 2
                    ps = slice(p0, p0 + DH)
                    q = qT[ps, m, q0:q0 + rows]
                    if t < 2:
                        segs = [(0, keys, kT[ps, m, 0:keys], ckT[p0:p0 + HEADS, 0:keys])]
                    else:
                        own = NP_TOK + PAST
                        segs = [(0, PAST, kcT[ps, m, :], ckT[p0:p0 + HEADS, NP_TOK:own]),
                                (PAST, keys, kT[ps, m, NP_TOK:NTOK], ckT[p0:p0 + HEADS, own:own + NS_TOK])]
                    for lo, hi, k, c in segs:
                        last = mm(bank[0:rows, lo:hi], q, k, start=True, stop=g == 1)
                        if g == 0:
                            of_h = ident[p0:p0 + HEADS, p0 + h:p0 + h + 1].to_broadcast([HEADS, rows])
                            last = mm(bank[0:rows, lo:hi], of_h, c, start=False, stop=True)
                    last.then_inc(sc_ready, 1)

                def turn(u):
                    h, t, keys = us[u]
                    n, rows = n0 + u, ROWS[t]
                    pe.wait_ge(exp_done, n + 1)
                    blocks = [(k, min(P, keys - k)) for k in range(0, keys, P)]
                    for g0 in range(0, len(blocks), 4):
                        bank = t_bank(tj[0])
                        for x, (k, w) in enumerate(blocks[g0:g0 + 4]):
                            last = nc.tensor.transpose(bank[0:w, x * P:x * P + rows], srow[0:rows, n % 2, k:k + w], ident[0:rows, 0:rows])
                        last.then_inc(t_ready, 1)
                        tj[0] += 1
                    ready_at[u] = tj[0]

                def values(u):
                    h, t, keys = us[u]
                    n, rows = n0 + u, ROWS[t]
                    pe.wait_ge(t_used, ready_at[u])
                    bank = a_bank(j0 + u)
                    nb = -(-keys // P)
                    for b in range(nb):
                        w = min(P, keys - b * P)
                        if g == 2:
                            src = (mv if t < 2 else cmv)[:, b, h * P:(h + 1) * P]
                        elif t == 2 and b < PB:
                            src = vc[:, b, h * DH:(h + 1) * DH]
                        else:
                            src = v[0:w, b if t < 2 else 2, h * DH:(h + 1) * DH]
                        last = mm(bank[0:rows, 0:P if g == 2 else DH], pT[0:w, n % 2, b, 0:rows], src, start=b == 0, stop=b == nb - 1)
                    last.then_inc(a_ready, 1)

                for s in range(len(us) + 2):
                    if s < len(us):
                        scores(s)
                    if 1 <= s <= len(us):
                        turn(s - 1)
                    if s >= 2:
                        values(s - 2)

            for g in range(2):
                j = A_GROUP[g]
                w = weights(J_Q + 3 * g)
                for m in range(M4):
                    by_weights(j + m, w, hT, NTOK, m)
                w = weights(J_K + 3 * g)
                for m in range(M4):
                    by_weights(j + 4 + m, w, hT, NTOK, m)
                w = weights(J_V + 3 * g)
                for t in range(TILES):
                    by_tokens(j + 8 + t, lambda c: hT[:, c, OFF[t]:OFF[t] + ROWS[t]], w, C, slice(0, 512), ROWS[t])
                if g == 0:
                    pe.wait_ge(small_in, SMALL)
                    bank = a_bank(A_FL)
                    for t in range(TILES):
                        for c in range(C):
                            last = mm(bank[0:ROWS[t], 8 * t:8 * t + 8], hT[:, c, OFF[t]:OFF[t] + ROWS[t]], wfl[:, c, :],
                                      start=c == 0, stop=c == C - 1)
                    last.then_inc(a_ready, 1)
                pe.wait_ge(stage_in[g], 16)
                for b in range(PB):
                    bank = t_bank(T_CACHE[g] + b)
                    for m in range(M4):
                        last = nc.tensor.transpose(bank[:, m * P:(m + 1) * P], stage[:, b, m * P:(m + 1) * P], ident[:, :])
                    last.then_inc(t_ready, 1)
                pe.wait_ge(a_used, j + 8)
                for t in range(TILES):
                    bank = t_bank(T_KBACK[g] + t)
                    for m in range(M4):
                        last = nc.tensor.transpose(bank[0:ROWS[t], m * P:(m + 1) * P], kT[:, m, OFF[t]:OFF[t] + ROWS[t]], ident[:, :])
                    last.then_inc(t_ready, 1)
                if g == 0:
                    pe.wait_ge(lf_ready, 1)

                    def cumulate(bank, c0, blocks, rows, heads_first):
                        for x, (lf, k) in enumerate(blocks):
                            last_one = x == len(blocks) - 1
                            m_ = (tri if last_one else ones)[0:k, 0:rows]
                            if heads_first:
                                r = mm(bank[0:8, c0:c0 + rows], lf, m_, start=x == 0, stop=last_one)
                            else:
                                r = mm(bank[0:rows, c0:c0 + 8], m_, lf, start=x == 0, stop=last_one)
                        return r

                    own = [(lfb[:, 0, :], P), (lfb[:, 1, :], P)]
                    past = [(clf[:, b, :], P) for b in range(PB)]
                    sample = past + [(lfb[0:NS_TOK, 2, :], NS_TOK)]
                    bank = a_bank(A_CTOK)
                    cumulate(bank, 0, own[:1], P, False)
                    cumulate(bank, 8, own, P, False)
                    cumulate(bank, 16, sample, NS_TOK, False).then_inc(a_ready, 1)
                    bank = a_bank(A_CPRO)
                    cumulate(bank, 0, own[:1], P, True)
                    cumulate(bank, P, own, P, True)
                    cumulate(bank, NP_TOK, sample, NS_TOK, True).then_inc(a_ready, 1)
                    bank = a_bank(A_CPAST)
                    for b in range(PB):
                        last = cumulate(bank, b * P, past[:b + 1], P, True)
                    last.then_inc(a_ready, 1)
                    pe.wait_ge(rel_in, 16)
                    for x in range(4):
                        bank = a_bank(A_REL + x)
                        for h in (2 * x, 2 * x + 1):
                            for kb in range(2):
                                c0 = 256 * (h % 2) + P * kb
                                last = mm(bank[:, c0:c0 + P], hankel[:, h, P * (1 - kb):P * (2 - kb)], anti[:, :], start=True, stop=True)
                        last.then_inc(a_ready, 1)
                pe.wait_ge(a_used, A_PV[g])
                pe.wait_ge(t_used, T_ATT[g])
                pe.wait_ge(vc_in[g], 16)
                attention(g, 24 * g, A_PV[g], T_ATT[g])

            for t in range(TILES):
                transpose_norm(N_MERGE + t, T_MERGE + 2 * t, ROWS[t])
            pe.wait_ge(t_used, T_MEM)
            w2 = [weights(J_WOUT), weights(J_WOUT + 1)]
            for t in range(TILES):
                for half in range(2):
                    by_tokens(A_WOUT + 2 * t + half, lambda c: hT[:, c, OFF[t]:OFF[t] + ROWS[t]], w2[half], C, slice(0, 512), ROWS[t])
            for t in range(MB):
                transpose_norm(N_MEM + t, T_MEM + 2 * t, P)
            pe.wait_ge(cmk_in, 16)
            for b in range(MB):
                bank = t_bank(T_CMK + b)
                for m in range(M4):
                    last = nc.tensor.transpose(bank[:, m * P:(m + 1) * P], ktok[:, b, m * P:(m + 1) * P], ident[:, :])
                last.then_inc(t_ready, 1)
            pe.wait_ge(t_used, T_MEM + 4)
            w = weights(J_CK)
            for m in range(HM):
                by_weights(A_MEM + m, w, memT, NMEM, m)
            w = weights(J_CV)
            for b in range(MB):
                by_tokens(A_MEM + HM + b, lambda c: memT[:, c, b * P:(b + 1) * P], w, C, slice(0, 512), P)
            pe.wait_ge(a_used, A_MEM + HM)
            for b in range(MB):
                bank = t_bank(T_MKBACK + b)
                for m in range(HM):
                    last = nc.tensor.transpose(bank[:, m * P:(m + 1) * P], mkT[:, m, b * P:(b + 1) * P], ident[:, :])
                last.then_inc(t_ready, 1)
            for t in range(TILES):
                transpose_norm(N_CROSS + t, T_CROSS + 2 * t, ROWS[t])
            pe.wait_ge(t_used, T_XATT)
            w = weights(J_CQ)
            for m in range(M4):
                by_weights(A_CQ + m, w, hT, NTOK, m)
            pe.wait_ge(a_used, A_XPV)
            pe.wait_ge(cmv_in, 16)
            attention(2, 48, A_XPV, T_XATT)
            pe.wait_ge(a_used, A_CO)
            for t in range(TILES):
                bank = t_bank(T_OX + t)
                for m in range(M4):
                    last = nc.tensor.transpose(bank[:, m * P:m * P + ROWS[t]], oall[0:ROWS[t], t, m * P:(m + 1) * P], ident[0:ROWS[t], 0:ROWS[t]])
                last.then_inc(t_ready, 1)
            pe.wait_ge(t_used, T_FFN)
            w = weights(J_CO)
            for t in range(TILES):
                for half in range(2):
                    by_tokens(A_CO + 2 * t + half, lambda c: hT[:, c, OFF[t]:OFF[t] + ROWS[t]], w, M4, slice(half * 512, half * 512 + 512), ROWS[t])
            for t in range(TILES):
                transpose_norm(N_FFN + t, T_FFN + 2 * t, ROWS[t])
            pe.wait_ge(t_used, T_FFN + 6)
            bank = a_bank(A_ROUTE)
            R = NG + NE
            for t in range(TILES):
                for c in range(C):
                    last = mm(bank[0:ROWS[t], R * t:R * t + R], hT[:, c, OFF[t]:OFF[t] + ROWS[t]], wr[:, c, :], start=c == 0, stop=c == C - 1)
            last.then_inc(a_ready, 1)
            pe.wait_ge(moh_ready, 1)
            bank = a_bank(A_POS)
            for t in range(TILES):
                for x in range(t + 1):
                    last_one = x == t
                    mm(bank[0:ROWS[t], NE * t:NE * t + NE], (stri if last_one else ones)[0:ROWS[x], 0:ROWS[t]],
                       mboth[0:ROWS[x], x, :], start=x == 0, stop=last_one)
            for t in range(TILES):
                last = mm(bank[:, NE * TILES:NE * (TILES + 1)], ones[0:ROWS[t], :], mboth[0:ROWS[t], t, :], start=t == 0, stop=t == 2)
            last.then_inc(a_ready, 1)
            pe.wait_ge(a_used, A_POS + 1)

            def transpose_rows(n, b):
                pe.wait_ge(xg_in[b], (n - b) * 8 + 16)
                pe.nop().then_inc(pe_passed, 1)
                src = xg[:, b, :].rearrange("s (p c) -> s c p", c=C)
                for c in range(C):
                    last = nc.tensor.transpose(pTr[b][:, c * SLOTS:(c + 1) * SLOTS], src[:, c, :], ident[0:SLOTS, 0:SLOTS])
                last.then_inc(xt_ready, 1)

            def gate_up(n, b):
                pe.wait_ge(xe_ready, n + 1)
                for x in range(2):
                    pe.wait_ge(w_in_s[3 * b + x], (n - b) * 8 + 48)
                    w = by_k(3 * b + x)
                    for f in range(FC):
                        for c in range(C):
                            last = mm(pA[b][:, x * 256 + f * SLOTS:x * 256 + (f + 1) * SLOTS], w[:, c, f * P:(f + 1) * P],
                                      xeT[:, b, c, :], start=c == 0, stop=c == C - 1)
                    last.then_inc(gu_ready if x else gate_read, 1)
                transpose_rows(n + 1, 1 - b)

            def down(n, b, first=False):
                pe.wait_ge(at_ready, n + 1)
                if not first:
                    pe.wait_ge(y_summed, n - 1)
                for f in range(FC):
                    a = a_split[:, b, f, :, :].rearrange("p k s -> p (k s)")
                    pe.wait_ge(w_lo_ready, n * FC + f + 1)
                    for half in range(2):
                        for part in (w_hi, w_lo):
                            last = mm(pS[b][:, half * 512:(half + 1) * 512], a, part[:, f, half * 512:(half + 1) * 512],
                                      start=f == 0 and part is w_hi, stop=f == FC - 1 and part is w_lo)
                last.then_inc(y_ready, 1)

            def experts(r):
                n = r * NE
                first = isinstance(r, int)
                gate_up(n, 0)
                for e in range(1, 4):
                    gate_up(n + e, e % 2)
                    down(n + e - 1, (e - 1) % 2, first and e < 3)
                with pe.Fori(2, NE // 2) as p:
                    gate_up(n + p * 2, 0)
                    down(n + p * 2 - 1, 1)
                    gate_up(n + p * 2 + 1, 1)
                    down(n + p * 2, 0)
                down(n + NE - 1, 1)

            transpose_rows(0, 0)
            experts(0)
            most = pe.value_load(cnti[0:1, 0:1], min_val=0, max_val=NTOK)
            with pe.If(most > SLOTS):
                with pe.Fori(1, ROUNDS) as r:
                    experts(r)

        @block.vector
        def _(dve):
            nv = nc.vector
            steps = [0]

            def step(ins):
                steps[0] += 1
                ins.then_inc(dve_step, 1)
                dve.wait_ge(dve_step, steps[0])

            nv.memset(flx[:, :], 0.0)
            nv.memset(lg[:, :, :], 0.0)
            nv.memset(posb[:, :, :], 0.0)
            nv.memset(lg8[:, :, :], -3e38).then_inc(consts, 1)
            dve.wait_ge(gmix_in, 16)

            def norm(j, rows, dstT, off, gain):
                for half in range(2):
                    dve.wait_ge(t_ready, j + half + 1)
                    src = pTr[(j + half) % 2][:, :].rearrange("p (c t) -> p c t", c=4)[:, :, 0:rows]
                    gg = gcol[:, gain, 4 * half:4 * half + 4].unsqueeze(2).to_broadcast([P, 4, rows])
                    nv.tensor_tensor(dstT[:, 4 * half:4 * half + 4, off:off + rows], src, gg, ALU.mult).then_inc(t_used, 1)

            for t in range(TILES):
                norm(T_MIX + 2 * t, ROWS[t], hT, OFF[t], 0)
            dve.wait_ge(rel_raw, 16)
            nv.tensor_copy(relT[:, 2 * CLIP + 1:384], relT[:, 2 * CLIP:2 * CLIP + 1].to_broadcast([HEADS, 127])).then_inc(rel_rows, 1)
            dve.wait_ge(small_in, SMALL)

            def attention(g, n0, j0, t0):
                us = units(g)
                tj = [t0]

                def scores(u):
                    h, t, keys = us[u]
                    n, rows = n0 + u, ROWS[t]
                    b = n % 2
                    dst, bank = srow[0:rows, b, :], pS[b][0:rows, :]
                    dve.wait_ge(sc_ready, n + 1)
                    if g == 0:
                        c = cq[0:rows, 8 * t + h:8 * t + h + 1]
                        if t == 2:
                            nv.tensor_scalar(dst[:, 0:PAST], bank[:, 0:PAST], c, None, ALU.add)
                            lo, mask = PAST, cmask[0:rows, P:P + NS_TOK]
                        else:
                            lo, mask = 0, cmask[:, 256 - keys:256]
                        ins = nv.scalar_tensor_tensor(dst[:, lo:keys], bank[:, lo:keys], c, mask, ALU.add, ALU.add)
                    elif g == 1:
                        if t == 2:
                            far = PAST - P
                            nv.tensor_scalar(dst[:, 0:far], bank[:, 0:far], t256[:, h:h + 1], None, ALU.add)
                            lo, bias = far, relb[0:rows, h, 0:keys - far]
                        else:
                            lo, bias = 0, relb[:, h, 256 - keys:256]
                        ins = nv.tensor_tensor(dst[:, lo:keys], bank[:, lo:keys], bias, ALU.add)
                    else:
                        ins = nv.tensor_scalar(dst[:, 0:keys], bank[:, 0:keys], MEM_SCALE, None, ALU.mult)
                    ins.then_inc(sc_used, 1)
                    dve.wait_ge(sc_used, n + 1)
                    nv.reduce_max(negmax[0:rows, b:b + 1], dst[:, 0:keys], AX.X, negate=True).then_inc(max_ready, 1)

                def turned(u):
                    h, t, keys = us[u]
                    n, rows = n0 + u, ROWS[t]
                    b = n % 2
                    dve.wait_ge(exp_done, n + 1)
                    if u >= 2:
                        dve.wait_ge(a_used, j0 + u - 1)
                    nv.reciprocal(rinv[0:rows, b:b + 1], rowsum[0:rows, b:b + 1]).then_inc(rinv_done, 1)
                    nb = -(-keys // P)
                    for b0 in range(0, nb, 4):
                        k = min(4, nb - b0)
                        w = min(P, keys - b0 * P)
                        dve.wait_ge(t_ready, tj[0] + 1)
                        src = pTr[tj[0] % 2][0:w, 0:k * P].rearrange("p (b q) -> p b q", q=P)[:, :, 0:rows]
                        nv.tensor_copy(pT[0:w, b, b0:b0 + k, 0:rows], src).then_inc(t_used, 1)
                        tj[0] += 1

                for s in range(len(us) + 1):
                    if s < len(us):
                        scores(s)
                    if s >= 1:
                        turned(s - 1)

            def to_cols(j, dst, rows=P, width=512):
                dve.wait_ge(t_ready, j + 1)
                nv.tensor_copy(dst, pTr[j % 2][0:rows, 0:width].rearrange("p (m k) -> p m k", m=4)).then_inc(t_used, 1)

            for g in range(2):
                if g == 0:
                    dve.wait_ge(a_used, A_FL + 1)
                    step(nv.tensor_tensor(flz[:, :].rearrange("p (t h) -> p t h", t=TILES), flx[:, :].rearrange("p (t h) -> p t h", t=TILES),
                                          bfb[:, :].unsqueeze(1).to_broadcast([P, TILES, HEADS]), ALU.add))
                    nv.scalar_tensor_tensor(fla[:, :], flz[:, :], -1.0, flz[:, :], ALU.mult, ALU.min).then_inc(z_ready, 1)
                for b in range(PB):
                    to_cols(T_CACHE[g] + b, kcT[:, :, b * P:(b + 1) * P])
                for t in range(TILES):
                    if g == 1:
                        dve.wait_ge(ktok_stored[t], 16)
                    dve.wait_ge(t_ready, T_KBACK[g] + t + 1)
                    nv.tensor_copy(ktok[0:ROWS[t], t, :], pTr[(T_KBACK[g] + t) % 2][0:ROWS[t], :]).then_inc(t_used, 1)
                if g == 0:
                    dve.wait_ge(ln_ready, 1)
                    nv.scalar_tensor_tensor(lfb[:, :, :].rearrange("p t h -> p (t h)"), flz[:, :], 0.0, fla[:, :], ALU.min, ALU.subtract).then_inc(lf_ready, 1)
                    dve.wait_ge(a_used, A_CTOK + 1)
                    dve.wait_ge(rel_in, 16)
                else:
                    dve.wait_ge(rel_ready, 1)
                attention(g, 24 * g, A_PV[g], T_ATT[g])

            def residual(j, t, half):
                rows = ROWS[t]
                dve.wait_ge(a_ready, j + 1)
                x = xres[0:rows, t, half * 512:(half + 1) * 512]
                nv.tensor_tensor(x, x, pA[j % 2][0:rows, :], ALU.add).then_inc(a_used, 1)

            for t in range(TILES):
                norm(T_MERGE + 2 * t, ROWS[t], hT, OFF[t], 1)
            for t in range(TILES):
                for half in range(2):
                    residual(A_WOUT + 2 * t + half, t, half)
            for t in range(MB):
                norm(T_MEM + 2 * t, P, memT, t * P, 2)
            for b in range(MB):
                to_cols(T_CMK + b, cmkT[:, :, b * P:(b + 1) * P])
            for b in range(MB):
                dve.wait_ge(t_ready, T_MKBACK + b + 1)
                nv.tensor_copy(mktok[:, b, :], pTr[(T_MKBACK + b) % 2][:, :]).then_inc(t_used, 1)
            for t in range(TILES):
                norm(T_CROSS + 2 * t, ROWS[t], hT, OFF[t], 3)
            attention(2, 48, A_XPV, T_XATT)
            for t in range(TILES):
                dve.wait_ge(t_ready, T_OX + t + 1)
                nv.tensor_copy(hT[:, 0:4, OFF[t]:OFF[t] + ROWS[t]],
                               pTr[(T_OX + t) % 2][:, :].rearrange("p (c t) -> p c t", c=4)[:, :, 0:ROWS[t]]).then_inc(t_used, 1)
            for t in range(TILES):
                for half in range(2):
                    residual(A_CO + 2 * t + half, t, half)
            for t in range(TILES):
                norm(T_FFN + 2 * t, ROWS[t], hT, OFF[t], 4)

            R = NG + NE
            dve.wait_ge(a_ready, A_ROUTE + 1)
            nv.tensor_tensor(lg[:, 0:2, :], pA[A_ROUTE % 2][:, 0:2 * R].rearrange("p (t r) -> p t r", t=2),
                             brb[:, :].unsqueeze(1).to_broadcast([P, 2, R]), ALU.add)
            nv.tensor_tensor(lg[0:64, 2, :], pA[A_ROUTE % 2][0:64, 2 * R:3 * R], brb[0:64, :], ALU.add).then_inc(a_used, 1)
            dve.wait_ge(a_used, A_ROUTE + 1)
            step(nv.tensor_copy(lg8[:, :, 0:NG], lg[:, :, 0:NG]))
            for t in range(TILES):
                ins = nv.max(top1[:, t, :], lg8[:, t, :])
            step(ins)
            nv.tensor_scalar(nm1[:, :], top1[:, :, 0], -1.0, None, ALU.mult).then_inc(top1_ready, 1)
            for t in range(TILES):
                ins = nv.max_index(top1i[:, t, :], top1[:, t, :], lg8[:, t, :])
            step(ins)
            step(nv.tensor_copy(gidx[:, :], top1i[:, :, 0]))
            step(nv.tensor_tensor(goh[:, :, :], iota32[:, 0:NG].unsqueeze(1).to_broadcast([P, TILES, NG]),
                                  gidx[:, :].unsqueeze(2).to_broadcast([P, TILES, NG]), ALU.is_equal))
            for t in range(TILES):
                ins = nv.tensor_tensor(l2m[:, t, :, :], lg[:, t, NG:].rearrange("p (g e) -> p g e", g=NG),
                                       goh[:, t, :].unsqueeze(2).to_broadcast([P, NG, EPG]), ALU.mult)
            step(ins)
            step(nv.reduce_sum(l2g[:, :, :], l2m[:, :, :, :].rearrange("p t g e -> p t e g"), AX.X))
            for t in range(TILES):
                ins = nv.max(top2[:, t, :], l2g[:, t, :])
            step(ins)
            nv.tensor_tensor(dlt[:, :], top2[:, :, 1], top2[:, :, 0], ALU.subtract).then_inc(dlt_ready, 1)
            for t in range(TILES):
                ins = nv.max_index(top2i[:, t, :], top2[:, t, :], l2g[:, t, :])
            step(ins)
            for k in range(2):
                ins = nv.tensor_copy(eid[:, k, :], top2i[:, :, k])
            step(ins)
            for k in range(2):
                ins = nv.scalar_tensor_tensor(eid[:, k, :], gidx[:, :], float(EPG), eid[:, k, :], ALU.mult, ALU.add)
            step(ins)
            for k in range(2):
                ins = nv.tensor_tensor(moh[:, k, :, :], iota32[:, :].unsqueeze(1).to_broadcast([P, TILES, NE]),
                                       eid[:, k, :].unsqueeze(2).to_broadcast([P, TILES, NE]), ALU.is_equal)
            step(ins)
            nv.tensor_tensor(mboth[:, :, :], moh[:, 0, :, :], moh[:, 1, :, :], ALU.add).then_inc(moh_ready, 1)
            dve.wait_ge(ex4_ready, 1)
            step(nv.reciprocal(s4[:, :], s4[:, :]))
            dve.wait_ge(edl_ready, 1)
            step(nv.tensor_scalar(gate[:, 0, :], edl[:, :], 1.0, None, ALU.add))
            step(nv.reciprocal(gate[:, 0, :], gate[:, 0, :]))
            step(nv.tensor_tensor(gate[:, 0, :], gate[:, 0, :], s4[:, :], ALU.mult))
            step(nv.tensor_tensor(gate[:, 1, :], gate[:, 0, :], edl[:, :], ALU.mult))
            dve.wait_ge(a_ready, A_POS + 1)
            bank = pA[A_POS % 2]
            nv.tensor_copy(posb[:, 0:2, :], bank[:, 0:2 * NE].rearrange("p (t e) -> p t e", t=2))
            nv.tensor_copy(posb[0:64, 2, :], bank[0:64, 2 * NE:3 * NE])
            nv.reduce_max(cnt[:, 0:1], bank[:, 3 * NE:4 * NE], AX.X).then_inc(a_used, 1)
            dve.wait_ge(a_used, A_POS + 1)
            nv.tensor_copy(cnti[:, :], cnt[:, 0:1])
            for t in range(TILES):
                ins = nv.scalar_tensor_tensor(keyb[:, t, :], posb[:, t, :], float(NE), iota32[:, :], ALU.mult, ALU.add)
            step(ins)
            for k in range(2):
                step(nv.tensor_tensor(kprod[:, :, :], keyb[:, :, :], moh[:, k, :, :], ALU.mult))
                step(nv.reduce_sum(keyf[:, k, :], kprod[:, :, :], AX.X))
            nv.tensor_copy(slot[:, :, :], keyf[:, :, :]).then_inc(slot_ready, 1)

            def rows_in(n, b):
                dve.wait_ge(xt_ready, n + 1)
                nv.tensor_tensor(xeT[:, b, :, :], pTr[b][:, :].rearrange("p (c s) -> p c s", c=C),
                                 gcol[:, 4, :].unsqueeze(2).to_broadcast([P, C, SLOTS]), ALU.mult).then_inc(xe_ready, 1)

            def activations(n, b, first=False):
                dve.wait_ge(sig_ready, n + 1)
                nv.tensor_tensor(sg[:, b, :], sg[:, b, :], pA[b][:, 0:256], ALU.mult).then_inc(a_split_step, 1)
                dve.wait_ge(a_split_step, n * 3 + 1)
                nv.tensor_tensor(aT[:, b, :], sg[:, b, :], pA[b][:, 256:512], ALU.mult).then_inc(a_split_step, 1)
                dve.wait_ge(a_split_step, n * 3 + 2)
                if not first:
                    dve.wait_ge(y_ready, n - 1)
                a = aT[:, b, :].rearrange("p (f s) -> p f s", f=FC)
                nv.tensor_copy(a_split[:, b, :, 0, :], a).then_inc(a_split_step, 1)
                dve.wait_ge(a_split_step, n * 3 + 3)
                nv.tensor_tensor(a_split[:, b, :, 1, :], a, a_split[:, b, :, 0, :].bitcast(F32), ALU.subtract).then_inc(at_ready, 1)
                rows_in(n + 1, 1 - b)

            def lower_weights(n, b):
                for f in range(FC):
                    dve.wait_ge(w_hi_ready, n * FC + f + 1)
                    nv.tensor_tensor(w_lo[:, f, :], by_k(3 * b + 2, FC)[:, f, :], w_hi[:, f, :].bitcast(F32), ALU.subtract).then_inc(w_lo_ready, 1)

            def sum_rows(n, b):
                dve.wait_ge(y_lower, n + 1)
                nv.tensor_tensor(ysb[:, b, :], ysb[:, b, :], pS[b][0:SLOTS, :], ALU.add).then_inc(y_summed, 1)

            def expert(n, b, first=False):
                activations(n, b, first)
                sum_rows(n - 1, 1 - b)
                lower_weights(n, b)

            def experts(r):
                n = r * NE
                first = isinstance(r, int)
                lower_weights(n, 0)
                activations(n, 0, first)
                expert(n + 1, 1, first)
                with dve.Fori(1, NE // 2) as p:
                    for b in range(2):
                        expert(n + p * 2 + b, b)
                sum_rows(n + NE - 1, 1)

            rows_in(0, 0)
            experts(0)
            most = dve.value_load(cnti[0:1, 0:1], min_val=0, max_val=NTOK)
            with dve.If(most > SLOTS):
                with dve.Fori(1, ROUNDS) as r:
                    experts(r)

            for t in range(TILES):
                rows = ROWS[t]
                dve.wait_ge(yg_in[t], 32)
                y0, y1, x = ygat[0:rows, t, 0, :], ygat[0:rows, t, 1, :], xres[0:rows, t, :]
                step(nv.tensor_scalar(y0, y0, gate[0:rows, 0, t:t + 1], None, ALU.mult))
                step(nv.scalar_tensor_tensor(y0, y1, gate[0:rows, 1, t:t + 1], y0, ALU.mult, ALU.add))
                nv.tensor_tensor(x, x, y0, ALU.add).then_inc(xfin_ready, 1)
            dve.wait_ge(gfin_in, 16)
            for t in range(TILES):
                rows, n = ROWS[t], N_FINAL + t
                dve.wait_ge(rstd_done, n + 1)
                nv.scalar_tensor_tensor(oall[0:rows, t, :], xres[0:rows, t, :], rstd[0:rows, 2 * n:2 * n + 1], gfin[0:rows, :], ALU.mult, ALU.mult).then_inc(yout_ready, 1)


SMALL = 13 * 16


def unit_rows(n):
    if N_MEM <= n < N_CROSS:
        return P
    return ROWS[(n if n < N_MEM else n - N_CROSS) % 3]


_INS = ["x_prompt", "x_sample", "cache_fox_k", "cache_fox_v", "cache_fox_logf", "cache_band_k", "cache_band_v",
        "cache_mem_k", "cache_mem_v", "mem_prompt", "g_mix", "w_in", "b_forget", "g_out_fox", "g_out_band", "rel_table",
        "w_out", "g_cross", "g_mem", "w_cq", "w_ck", "w_cv", "w_co", "g_ffn", "w_router1", "b_router1", "w_router2",
        "b_router2", "w_exp_gate", "w_exp_up", "w_exp_down", "g_final"]
_OUTS = [("y_prompt", (1, 256, 1024)), ("y_sample", (1, 64, 1024)),
         ("fox_k_p", (1, 1, 256, 8, 64)), ("fox_v_p", (1, 1, 256, 8, 64)), ("fox_logf_p", (1, 1, 256, 8)),
         ("band_k_p", (1, 1, 256, 8, 64)), ("band_v_p", (1, 1, 256, 8, 64)),
         ("mem_k_p", (1, 1, 256, 4, 128)), ("mem_v_p", (1, 1, 256, 4, 128)),
         ("fox_k_s", (1, 1, 64, 8, 64)), ("fox_v_s", (1, 1, 64, 8, 64)), ("fox_logf_s", (1, 1, 64, 8)),
         ("band_k_s", (1, 1, 512, 8, 64)), ("band_v_s", (1, 1, 512, 8, 64))]


def kernel(**inputs):
    import numpy as np
    import concourse.bacc as bacc
    from concourse.bass_utils import run_bass_kernel_spmd

    nc = bacc.Bacc("TRN2", target_bir_lowering=False, num_devices=1)
    arrays, ins, outs = {}, {}, {}
    for name in _INS:
        a = np.ascontiguousarray(inputs[name])
        arrays[f"in_{name}"] = a
        ins[name] = nc.dram_tensor(f"in_{name}", a.shape, mybir.dt.from_np(a.dtype), kind="ExternalInput").ap()
    for name, shape in _OUTS:
        outs[name] = nc.dram_tensor(f"out_{name}", shape, F32, kind="ExternalOutput").ap()
    build(nc, ins, outs)
    r = run_bass_kernel_spmd(nc, [arrays], core_ids=[0])
    return tuple(r.results[0][f"out_{name}"] for name, _ in _OUTS)
```

```python
from contextlib import ExitStack

import concourse.bass as bass
from concourse import mybir

F32 = mybir.dt.float32
F32R = mybir.dt.float32r
U32 = mybir.dt.uint32
I32 = mybir.dt.int32
ALU = mybir.AluOpType
ACT = mybir.ActivationFunctionType
AX = mybir.AxisListType

P = 128
D = 1024
C = D // P
NP_TOK, NS_TOK = 256, 64
NTOK = NP_TOK + NS_TOK
TILES = 3
ROWS = [128, 128, 64]
OFF = [0, 128, 256]
HEADS, DH = 8, 64
W = HEADS * DH
M4 = W // P
PAST = 512
PB = PAST // P
CLIP = 128
NMEM, HM = 256, 4
MB = NMEM // P
NG, EPG = 4, 8
NE = NG * EPG
DE = 512
FC = DE // P
SLOTS = 64
ROUNDS = NTOK // SLOTS
GW = FC * SLOTS
RING = 6
EPS = 1e-6
NEG = -1e30
Q_SCALE = DH ** -0.5
MEM_SCALE = 128 ** -0.5

A_GROUP = [0, 43]
A_FL, A_REL, A_CTOK, A_CPRO, A_CPAST = 11, 12, 16, 17, 18
A_PV = [19, 54]
A_WOUT = 78
A_MEM = 84
A_CQ = 90
A_XPV = 94
A_CO = 106
A_ROUTE = 112
A_POS = 113
A_LIST = 114
T_MIX = 0
T_CACHE = [6, 45]
T_KBACK = [10, 49]
T_ATT = [13, 52]
T_MERGE = 84
T_MEM = 90
T_CMK = 94
T_CROSS = 96
T_MKBACK = 102
T_XATT = 104
T_OX = 116
T_FFN = 119
N_MIX, N_MERGE, N_MEM, N_CROSS, N_FFN, N_FINAL = 0, 3, 6, 8, 11, 14


def build(nc, i, o):
    with ExitStack() as ctx:
        def sb(name, shape, dt=F32):
            return ctx.enter_context(nc.sbuf_tensor(name, shape, dt))

        def sem(name):
            return ctx.enter_context(nc.semaphore(name))

        def dram(name, shape, dt=F32):
            return nc.dram_tensor(name, shape, dt, kind="Internal").ap()

        ring = [sb(f"ring{s}", [P, 4096]) for s in range(RING)]
        xres = sb("xres", [P, TILES, D])
        srow = sb("srow", [P, 2, PAST + NS_TOK])
        pT = sb("pT", [P, 2, 5, P])
        zone = sb("zone", [P, 8192])

        kcT = zone[:, 0:2048].rearrange("p (m k) -> p m k", m=M4)
        vc = zone[:, 2048:4096].rearrange("p (b w) -> p b w", b=PB)
        qT = zone[:, 4096:5376].rearrange("p (m t) -> p m t", m=M4)
        kT = zone[:, 5376:6656].rearrange("p (m t) -> p m t", m=M4)
        v = zone[:, 6656:8192].rearrange("p (t w) -> p t w", t=TILES)

        xmem = zone[:, 0:2048].rearrange("p (t d) -> p t d", t=MB)
        mktok = zone[:, 0:1024].rearrange("p (t w) -> p t w", t=MB)
        memT = zone[:, 2048:4096].rearrange("p (c t) -> p c t", c=C)
        cmv = zone[:, 4096:5120].rearrange("p (b w) -> p b w", b=MB)
        cmkT = zone[:, 5120:6144].rearrange("p (m k) -> p m k", m=HM)
        mkT = zone[:, 6144:7168].rearrange("p (m k) -> p m k", m=HM)
        mv = zone[:, 7168:8192].rearrange("p (b w) -> p b w", b=MB)

        xg = zone[0:SLOTS, 0:2048].rearrange("p (b d) -> p b d", b=2)
        xeT = zone[:, 2048:2048 + 2 * C * SLOTS].rearrange("p (b c s) -> p b c s", b=2, c=C)
        aT = zone[:, 3072:3072 + 2 * GW].rearrange("p (b f) -> p b f", b=2)
        sg = zone[:, 3584:3584 + 2 * GW].rearrange("p (b f) -> p b f", b=2)
        ysb = zone[0:SLOTS, 4096:6144].rearrange("p (b d) -> p b d", b=2)
        ygat = zone[:, 0:6144].rearrange("p (t k d) -> p t k d", t=TILES, k=2)
        gfin = zone[:, 6144:7168]

        ident = sb("ident", [P, P])
        anti = sb("anti", [P, P])
        tri = sb("tri", [P, P])
        stri = sb("stri", [P, P])
        ones = sb("ones", [P, P])
        cmask = sb("cmask", [P, 256])
        mhalf = sb("mhalf", [P, 2])
        iota32 = sb("iota32", [P, NE])
        iota_slot = sb("iota_slot", [P, SLOTS])
        tokf = sb("tokf", [P, TILES])
        tokid = sb("tokid", [P, TILES], U32)
        zero_u = sb("zero_u", [P, NTOK * NE // P], U32)
        gcol = sb("gcol", [P, 5, C])
        bfb = sb("bfb", [P, HEADS])
        wfl = sb("wfl", [P, C, HEADS])
        wr = sb("wr", [P, C, NG + NE])
        brb = sb("brb", [P, NG + NE])
        relT = pT[0:HEADS, 1, 0:3, :].rearrange("p b q -> p (b q)")
        t256 = sb("t256", [NS_TOK, HEADS])
        ss = sb("ss", [P, 2 * 17])
        ms = sb("ms", [P, 2 * 17])
        rstd = sb("rstd", [P, 2 * 17])
        flx = sb("flx", [P, 24])
        flz = sb("flz", [P, 24])
        fla = sb("fla", [P, 24])
        lfb = sb("lfb", [P, TILES, HEADS])
        clf = sb("clf", [P, PB, HEADS])
        clfpad = srow[:, 0, 0:PB * P].rearrange("p (b w) -> p b w", b=PB)
        lfpad = srow[:, 1, 0:TILES * P].rearrange("p (t w) -> p t w", t=TILES)
        selr = sb("selr", [P, HEADS], F32R)
        cq = sb("cq", [P, 24])
        ckT = sb("ckT", [P, NP_TOK + PAST + NS_TOK], F32R)
        negmax = sb("negmax", [P, TILES])
        rowsum = sb("rowsum", [P, TILES])
        rinv = sb("rinv", [P, TILES])
        route = pT[:, 0, :, :].rearrange("p b q -> p (b q)")
        lg = sb("lg", [P, TILES, NG + NE])
        lg8 = sb("lg8", [P, TILES, 8])
        top1 = sb("top1", [P, TILES, 8])
        top1i = sb("top1i", [P, TILES, 8], U32)
        nm1 = sb("nm1", [P, TILES])
        ex4 = sb("ex4", [P, TILES, NG])
        s4 = sb("s4", [P, TILES])
        gidx = sb("gidx", [P, TILES])
        goh = sb("goh", [P, TILES, NG])
        l2m = route[:, 0:96].rearrange("p (t g e) -> p t g e", t=TILES, g=NG)
        l2g = sb("l2g", [P, TILES, EPG])
        top2 = sb("top2", [P, TILES, 8])
        top2i = sb("top2i", [P, TILES, 8], U32)
        dlt = sb("dlt", [P, TILES])
        edl = sb("edl", [P, TILES])
        gate = sb("gate", [P, 2, TILES])
        eid = sb("eid", [P, 2, TILES])
        moh = route[:, 96:288].rearrange("p (k t e) -> p k t e", k=2, t=TILES)
        mboth = route[:, 288:384].rearrange("p (t e) -> p t e", t=TILES)
        posb = sb("posb", [P, TILES, NE])
        keyb = route[:, 384:480].rearrange("p (t e) -> p t e", t=TILES)
        kprod = route[:, 480:576].rearrange("p (t e) -> p t e", t=TILES)
        keyf = sb("keyf", [P, 2, TILES])
        place2 = sb("place2", [P, TILES, 2])
        in_place = pT[:, 1, :, :].rearrange("p b q -> p (b q)")[:, 0:TILES * 2 * SLOTS].rearrange("p (t e s) -> p t e s", t=TILES, e=2)
        slot = sb("slot", [P, 2, TILES], U32)
        cnt = sb("cnt", [P, 1])
        cnti = sb("cnti", [P, 1], I32)
        idx_all = srow[0:SLOTS, 0, 0:ROUNDS * NE + 2].bitcast(U32)
        idx_cur = [sb(f"idx_cur{b}", [SLOTS, 1], U32) for b in range(2)]

        with ExitStack() as front:
            def fsb(name, shape):
                return front.enter_context(nc.sbuf_tensor(name, shape, F32))

            hT = fsb("hT", [P, C, NTOK])
            hn = fsb("hn", [P, 2, D])
            oall = fsb("oall", [P, TILES, D])
            ktok = fsb("ktok", [P, TILES, W])
            relb = fsb("relb", [P, HEADS, 256])
        stage = hn[:, :, :].rearrange("p a (b w) -> p (a b) w", w=W)
        hankel = oall[:, 0:2, :].rearrange("p t (h j) -> p (t h) j", j=256)
        qxT = relb[:, :, :].rearrange("p h k -> p (h k)")[:, 0:M4 * NTOK].rearrange("p (m t) -> p m t", m=M4)
        w_hi = sb("w_hi", [P, FC, D], F32R)
        w_lo = sb("w_lo", [P, FC, D], F32R)
        a_split = sb("a_split", [P, 2, FC, 2, SLOTS], F32R)

        pA = [ctx.enter_context(nc.psum_tensor(f"pA{b}", [P, 512], F32)) for b in range(2)]
        pTr = [ctx.enter_context(nc.psum_tensor(f"pTr{b}", [P, 512], F32)) for b in range(2)]
        pS = [ctx.enter_context(nc.psum_tensor(f"pS{b}", [P, 1024], F32)) for b in range(2)]

        score_banks = [pS[1][:, 512:1024], pS[1][:, 0:512], pS[0][:, :]]
        flat_s = srow[:, :, :].rearrange("p b k -> p (b k)")
        srow_t = [flat_s[:, 0:256], flat_s[:, 256:512], flat_s[:, 512:512 + PAST + NS_TOK]]
        flat_p = pT[:, :, :, :].rearrange("p a b q -> p (a b) q")
        pT_t = [flat_p[:, 0:2, :], flat_p[:, 2:4, :], flat_p[:, 4:9, :]]

        relT_d = dram("relT_d", [HEADS, 384])
        hn_d = dram("hn_d", [NTOK, D])
        slot_d = dram("slot_d", [NTOK * NE, 1], U32)
        y_d = dram("y_d", [NTOK * NE, D])

        x_in = [sem(f"x_in{t}") for t in range(TILES)]
        gmix_in = sem("gmix_in")
        small_in = sem("small_in")
        rel_raw = sem("rel_raw")
        rel_rows = sem("rel_rows")
        rel_stored = sem("rel_stored")
        rel_in = sem("rel_in")
        rel_ready = sem("rel_ready")
        clf_in = sem("clf_in")
        stage_in = [sem(f"stage_in{g}") for g in range(2)]
        vc_in = [sem(f"vc_in{g}") for g in range(2)]
        xmem_in = sem("xmem_in")
        cmk_in = sem("cmk_in")
        cmv_in = sem("cmv_in")
        gfin_in = sem("gfin_in")
        w_in_s = [sem(f"w_loaded{s}") for s in range(RING)]
        gate_read = sem("gate_read")
        pe_passed = sem("pe_passed")
        pool_passed = sem("pool_passed")
        consts = sem("consts")
        pool_step = sem("pool_step")
        dve_step = sem("dve_step")
        act_step = sem("act_step")
        sq_done = sem("sq_done")
        rstd_done = sem("rstd_done")
        hn_ready = sem("hn_ready")
        hn_stored = [sem(f"hn_stored{t}") for t in range(TILES)]
        a_ready = sem("a_ready")
        a_used = sem("a_used")
        t_ready = sem("t_ready")
        t_used = sem("t_used")
        z_ready = sem("z_ready")
        ln_ready = sem("ln_ready")
        lf_ready = sem("lf_ready")
        lfpad_ready = sem("lfpad_ready")
        ck_hi = sem("ck_hi")
        sc_ready = sem("sc_ready")
        sc_used = sem("sc_used")
        max_ready = sem("max_ready")
        exp_done = sem("exp_done")
        rinv_done = sem("rinv_done")
        ktok_stored = [sem(f"ktok_stored{t}") for t in range(TILES)]
        v_stored = sem("v_stored")
        mk_stored = sem("mk_stored")
        out_stored = sem("out_stored")
        top1_ready = sem("top1_ready")
        ex4_ready = sem("ex4_ready")
        dlt_ready = sem("dlt_ready")
        edl_ready = sem("edl_ready")
        moh_ready = sem("moh_ready")
        slot_ready = sem("slot_ready")
        slot_zeroed = sem("slot_zeroed")
        slot_stored = sem("slot_stored")
        idx_in = sem("idx_in")
        place2_ready = sem("place2_ready")
        in_place_ready = sem("in_place_ready")
        idx_copied = sem("idx_copied")
        xg_in = [sem(f"xg_in{b}") for b in range(2)]
        xt_ready = sem("xt_ready")
        xe_ready = sem("xe_ready")
        gu_ready = sem("gu_ready")
        sig_ready = sem("sig_ready")
        at_ready = sem("at_ready")
        y_ready = sem("y_ready")
        w_hi_ready = sem("w_hi_ready")
        w_lo_ready = sem("w_lo_ready")
        a_split_step = sem("a_split_step")
        y_lower = sem("y_lower")
        y_summed = sem("y_summed")
        y_stored = [sem(f"y_stored{b}") for b in range(2)]
        moe_done = sem("moe_done")
        other_stored = sem("other_stored")
        yg_in = [sem(f"yg_in{t}") for t in range(TILES)]
        xfin_ready = sem("xfin_ready")
        yout_ready = sem("yout_ready")

        xp_d = i["x_prompt"][0].rearrange("(t p) d -> p t d", p=P)
        xs_d = i["x_sample"][0]
        w_in = i["w_in"][0].rearrange("(p c) n -> p c n", c=C)
        w_out = i["w_out"][0].rearrange("(p c) n -> p c n", c=C)
        flat = "t h d -> t (h d)"
        cache_k = [i["cache_fox_k"][0, 0].rearrange(flat), i["cache_band_k"][0, 0].rearrange(flat)]
        cache_v = [i["cache_fox_v"][0, 0].rearrange(flat), i["cache_band_v"][0, 0].rearrange(flat)]
        k_p = [o["fox_k_p"][0, 0].rearrange(flat), o["band_k_p"][0, 0].rearrange(flat)]
        v_p = [o["fox_v_p"][0, 0].rearrange(flat), o["band_v_p"][0, 0].rearrange(flat)]
        new = PAST - NS_TOK
        k_s = [o["fox_k_s"][0, 0].rearrange(flat), o["band_k_s"][0, 0].rearrange(flat)[new:, :]]
        v_s = [o["fox_v_s"][0, 0].rearrange(flat), o["band_v_s"][0, 0].rearrange(flat)[new:, :]]

        def cols(w, n):
            return w[:, :, n * 512:(n + 1) * 512]

        front_weights = [cols(w_in, 0), cols(w_in, 1), cols(w_in, 2), cols(w_in, 3), cols(w_in, 4), cols(w_in, 5),
                         cols(w_out, 0), cols(w_out, 1),
                         i["w_ck"][0].rearrange("(p c) n -> p c n", c=C),
                         i["w_cv"][0].rearrange("(p c) n -> p c n", c=C),
                         i["w_cq"][0].rearrange("(p c) n -> p c n", c=C),
                         i["w_co"][0].rearrange("(c p) n -> p c n", p=P)]
        assert len(front_weights) == 2 * RING
        a_done = [4, 8, 11, A_GROUP[1] + 4, A_GROUP[1] + 8, A_GROUP[1] + 11, A_WOUT + 6, A_WOUT + 6,
                  A_MEM + HM, A_MEM + HM + MB, A_CQ + M4, A_CO + 6]
        J_Q, J_K, J_V, J_WOUT, J_CK, J_CV, J_CQ, J_CO = 0, 1, 2, 6, 8, 9, 10, 11

        def by_k(j, k=C):
            return ring[j % RING][:, :].rearrange("p (c n) -> p c n", c=k)

        t_of = [T_MIX + 2 * t for t in range(3)] + [T_MERGE + 2 * t for t in range(3)] + [T_MEM, T_MEM + 2] \
            + [T_CROSS + 2 * t for t in range(3)] + [T_FFN + 2 * t for t in range(3)]

        def units(g):
            if g < 2:
                return [(h, t, [128, 256, PAST + NS_TOK][t]) for h in range(HEADS) for t in range(TILES)]
            return [(h, t, NMEM) for h in range(HM) for t in range(TILES)]

        own = NP_TOK + PAST
        CK_PARTS = [(A_CPRO, 0, NP_TOK, 0), (A_CPRO, own, own + NS_TOK, NP_TOK), (A_CPAST, NP_TOK, own, 0)]

        block = ctx.enter_context(nc.Block())

        @block.sync
        def _(sp):
            def load_weights(j):
                if j >= RING:
                    sp.wait_ge(a_ready, a_done[j - RING])
                sp.dma_start(by_k(j, front_weights[j].shape[1]), front_weights[j]).then_inc(w_in_s[j % RING], 16)

            for t in range(2):
                sp.dma_start(xres[:, t, :], xp_d[:, t, :]).then_inc(x_in[t], 16)
            sp.dma_start(xres[0:NS_TOK, 2, :], xs_d).then_inc(x_in[2], 16)
            load_weights(0)
            load_weights(1)
            small = 0
            for dst, src in ((gcol[0:64, 1, :], i["g_out_fox"][0].rearrange("(p c) -> p c", c=C)),
                             (gcol[64:128, 1, :], i["g_out_band"][0].rearrange("(p c) -> p c", c=C)),
                             (gcol[:, 2, :], i["g_mem"][0].rearrange("(p c) -> p c", c=C)),
                             (gcol[:, 3, :], i["g_cross"][0].rearrange("(p c) -> p c", c=C)),
                             (gcol[:, 4, :], i["g_ffn"][0].rearrange("(p c) -> p c", c=C)),
                             (wfl[:, :, :], w_in[:, :, 6 * W:6 * W + HEADS]),
                             (bfb[:, :], i["b_forget"][0].partition_broadcast(P)),
                             (t256[:, :], i["rel_table"][0, 2 * CLIP].partition_broadcast(NS_TOK)),
                             (wr[:, :, 0:NG], i["w_router1"][0].rearrange("(p c) n -> p c n", c=C)),
                             (wr[:, :, NG:], i["w_router2"][0].rearrange("(p c) n -> p c n", c=C)),
                             (brb[:, 0:NG], i["b_router1"][0].partition_broadcast(P)),
                             (brb[:, NG:], i["b_router2"][0].partition_broadcast(P)),
                             (clf[:, :, :], i["cache_fox_logf"][0, 0].rearrange("(b p) h -> p b h", p=P))):
                sp.dma_start(dst, src).then_inc(small_in, 16)
                small += 16
            assert small == SMALL
            table = i["rel_table"][0]
            with nc.allow_non_contiguous_dma(reason="the table by heads"):
                sp.dma_start(relT[:, 0:2 * CLIP + 1], table.rearrange("r h -> h r")).then_inc(rel_raw, 16)
            load_weights(2)
            sp.wait_ge(t_ready, T_MIX + 6)
            sp.dma_start(stage, cache_k[0].rearrange("(b p) w -> p b w", p=P)).then_inc(stage_in[0], 16)
            sp.dma_start(vc, cache_v[0].rearrange("(b p) w -> p b w", p=P)).then_inc(vc_in[0], 16)
            load_weights(3)
            load_weights(4)
            load_weights(5)
            sp.wait_ge(t_ready, T_CACHE[0] + 4)
            sp.dma_start(stage, cache_k[1].rearrange("(b p) w -> p b w", p=P)).then_inc(stage_in[1], 16)
            load_weights(6)
            load_weights(7)
            load_weights(8)
            sp.wait_ge(a_ready, A_PV[0] + 24)
            sp.dma_start(vc, cache_v[1].rearrange("(b p) w -> p b w", p=P)).then_inc(vc_in[1], 16)
            load_weights(9)
            load_weights(10)
            load_weights(11)
            sp.wait_ge(a_ready, A_PV[1] + 24)
            sp.dma_start(xmem, i["mem_prompt"][0].rearrange("(t p) d -> p t d", p=P)).then_inc(xmem_in, 16)
            sp.dma_start(cmv, i["cache_mem_v"][0, 0].rearrange("(b p) h d -> p b (h d)", p=P)).then_inc(cmv_in, 16)
            for t in range(TILES):
                sp.wait_ge(ktok_stored[t], 32)
            sp.dma_start(ktok[:, 0:MB, :], i["cache_mem_k"][0, 0].rearrange("(b p) h d -> p b (h d)", p=P)).then_inc(cmk_in, 16)

            def expert_weights(r, e, b, n, first=False):
                s = 3 * b + n
                if first:
                    sp.wait_ge(a_ready, a_done[RING + s])
                elif n < 2:
                    sp.wait_ge((gate_read, gu_ready)[n], r * NE + e - 1)
                else:
                    sp.wait_ge(w_lo_ready, (r * NE + e - 1) * FC)
                name = ("w_exp_gate", "w_exp_up", "w_exp_down")[n]
                if isinstance(e, int):
                    src = i[name][0, e]
                else:
                    src = i[name][0, bass.ds(e, 1)].rearrange("a k n -> (a k) n")
                if n < 2:
                    dst, src = by_k(s), src.rearrange("(p c) n -> p c n", c=C)
                else:
                    dst, src = by_k(s, FC), src.rearrange("(c p) n -> p c n", p=P)
                sp.dma_start(dst, src).then_inc(w_in_s[s], 16)

            def pair(r, p, first=False):
                for b in range(2):
                    for n in range(3):
                        expert_weights(r, 2 * p + b, b, n, first)

            def last_pair(r):
                for b, n in ((0, 0), (0, 1), (1, 0), (0, 2), (1, 1), (1, 2)):
                    expert_weights(r, NE - 2 + b, b, n)

            pair(0, 0, True)
            sp.dma_start(gfin, i["g_final"].partition_broadcast(P)).then_inc(gfin_in, 16)
            with sp.Fori(1, NE // 2 - 1) as p:
                pair(0, p)
            last_pair(0)
            sp.wait_ge(slot_ready, 1)
            most = sp.value_load(cnti[0:1, 0:1], min_val=0, max_val=NTOK)
            with sp.If(most > SLOTS):
                with sp.Fori(1, ROUNDS) as r:
                    with sp.Fori(0, NE // 2) as p:
                        pair(r, p)
            for t in range(TILES):
                sp.wait_ge(yout_ready, t + 1)
                dst = o["y_prompt"][0, t * P:(t + 1) * P, :] if t < 2 else o["y_sample"][0]
                sp.dma_start(dst, oall[0:ROWS[t], t, :]).then_inc(out_stored, 16)
            sp.wait_ge(out_stored, 16 * TILES)

        @block.gpsimd
        def _(pool):
            steps = [0]

            def step(ins):
                steps[0] += 1
                ins.then_inc(pool_step, 1)
                pool.wait_ge(pool_step, steps[0])

            pool.memset(ident[:, :], 0.0)
            pool.memset(anti[:, :], 0.0)
            pool.memset(ones[:, :], 1.0)
            pool.memset(cmask[:, :], 0.0)
            pool.memset(mhalf[:, :], -0.5)
            step(pool.memset(zero_u[:, :], 0))
            pool.dma_start(slot_d.rearrange("(p n) a -> p (n a)", p=P), zero_u[:, :]).then_inc(slot_zeroed, 16)
            pool.affine_select(out=ident[:, :], in_=ident[:, :], compare_op=ALU.not_equal, fill=1.0, base=0,
                               pattern=[[-1, P]], channel_multiplier=1)
            pool.affine_select(out=anti[:, :], in_=anti[:, :], compare_op=ALU.not_equal, fill=1.0, base=1 - P,
                               pattern=[[1, P]], channel_multiplier=1)
            pool.affine_select(out=tri[:, :], in_=ones[:, :], compare_op=ALU.is_ge, fill=0.0, base=0,
                               pattern=[[1, P]], channel_multiplier=-1)
            pool.affine_select(out=stri[:, :], in_=ones[:, :], compare_op=ALU.is_ge, fill=0.0, base=-1,
                               pattern=[[1, P]], channel_multiplier=-1)
            pool.affine_select(out=cmask[:, :], in_=cmask[:, :], compare_op=ALU.is_ge, fill=NEG, base=P,
                               pattern=[[-1, 256]], channel_multiplier=1)
            pool.iota(tokid[:, :], pattern=[[P, TILES]], base=0, channel_multiplier=1)
            pool.iota(iota32[:, :], pattern=[[1, NE]], base=0, channel_multiplier=0,
                      allow_small_or_imprecise_dtypes=True)
            pool.iota(iota_slot[:, :], pattern=[[1, SLOTS]], base=1, channel_multiplier=0,
                      allow_small_or_imprecise_dtypes=True)
            pool.iota(tokf[:, :], pattern=[[P, TILES]], base=0, channel_multiplier=1,
                      allow_small_or_imprecise_dtypes=True).then_inc(consts, 1)

            def rsqrt(n, two=False, width=D):
                rows = slice(0, unit_rows(n))
                cs = slice(2 * n, 2 * n + (2 if two else 1))
                pool.wait_ge(sq_done, n + 1)
                step(pool.tensor_scalar(ms[rows, cs], ss[rows, cs], 1.0 / width, EPS, ALU.mult, ALU.add))
                pool.tensor_tensor(rstd[rows, cs], ms[rows, cs], mhalf[rows, 0:2 if two else 1],
                                   ALU.pow).then_inc(rstd_done, 1)

            stores = [0]

            def store(dst, src, s=None, wait=None):
                if s is None:
                    stores[0] += 1
                pool.dma_start(dst, src).then_inc(s if s is not None else other_stored, 16)

            for n in range(N_MIX, N_MIX + 3):
                rsqrt(n)
            pool.wait_ge(rel_rows, 1)
            pool.dma_start(relT_d, relT).then_inc(rel_stored, 16)
            pool.wait_ge(rel_stored, 16)
            rows = bass.AP(tensor=relT_d.tensor, offset=1, ap=[[1, P], [384, HEADS], [1, 256]])
            pool.dma_start(hankel, rows).then_inc(rel_in, 16)
            store(o["band_k_s"][0, 0].rearrange(flat)[0:new, :], cache_k[1][NS_TOK:, :])
            store(o["band_v_s"][0, 0].rearrange(flat)[0:new, :], cache_v[1][NS_TOK:, :])
            for g in range(2):
                if g == 1:
                    pool.wait_ge(a_used, A_REL + 4)
                    pool.memset(relb[0:64, :, 192:256], NEG).then_inc(rel_ready, 1)
                for t in range(TILES):
                    pool.wait_ge(t_used, T_KBACK[g] + t + 1)
                    dst = k_p[g][t * P:(t + 1) * P, :] if t < 2 else k_s[g]
                    store(dst, ktok[0:ROWS[t], t, :], ktok_stored[t])
                pool.wait_ge(a_used, A_GROUP[g] + 11)
                store(v_p[g].rearrange("(t p) w -> p t w", p=P), v[:, 0:2, :], v_stored)
                store(v_s[g], v[0:NS_TOK, 2, :], v_stored)
                if g == 0:
                    pool.wait_ge(lf_ready, 1)
                    store(o["fox_logf_p"][0, 0].rearrange("(t p) h -> p t h", p=P), lfb[:, 0:2, :])
                    store(o["fox_logf_s"][0, 0], lfb[0:NS_TOK, 2, :])
            for n in range(N_MERGE, N_MERGE + 3):
                rsqrt(n, True, W)
            for n in range(N_MEM, N_MEM + 2):
                rsqrt(n)
            for n in range(N_CROSS, N_CROSS + 3):
                rsqrt(n)
            pool.wait_ge(t_used, T_MKBACK + 2)
            store(o["mem_k_p"][0, 0].rearrange("(b p) h d -> p b (h d)", p=P), mktok, mk_stored)
            pool.wait_ge(a_used, A_MEM + 6)
            store(o["mem_v_p"][0, 0].rearrange("(b p) h d -> p b (h d)", p=P), mv, mk_stored)
            for t in range(TILES):
                rsqrt(N_FFN + t)
                pool.wait_ge(hn_ready, N_FFN + t + 1)
                store(hn_d[OFF[t]:OFF[t] + ROWS[t], :], hn[0:ROWS[t], (N_FFN + t) % 2, :], hn_stored[t])

            def gather(n, b, first=False):
                if first:
                    pool.wait_ge(a_used, A_LIST + 1)
                else:
                    pool.wait_ge(xt_ready, n - 1)
                    pool.tensor_copy(idx_cur[b][:, :], idx_all[:, bass.ds(n, 1)]).then_inc(idx_copied, 1)
                    pool.wait_ge(idx_copied, n - 1)
                pool.nop().then_inc(pool_passed, 1)
                pool.indirect_dma_start(out=xg[:, b, :], out_offset=None, in_=hn_d,
                                        in_offset=bass.IndirectOffsetOnAxis(ap=idx_cur[b][:, :], axis=0)).then_inc(xg_in[b], 16)

            def take_rows(table, experts):
                pool.wait_ge(moe_done, 1)
                pool.wait_ge(xe_ready, experts + 2)
                for t in range(TILES):
                    for k in range(2):
                        pool.indirect_dma_start(out=ygat[0:ROWS[t], t, k, :], out_offset=None, in_=table,
                                                in_offset=bass.IndirectOffsetOnAxis(ap=slot[0:ROWS[t], k, t:t + 1], axis=0)).then_inc(yg_in[t], 16)

            for t in range(TILES):
                pool.wait_ge(hn_stored[t], 16)
            pool.wait_ge(mk_stored, 32)
            gather(0, 0, True)
            gather(1, 1, True)
            step(pool.memset(idx_all[:, ROUNDS * NE:], 0))
            pool.wait_ge(slot_ready, 1)
            pool.wait_ge(slot_zeroed, 16)
            for t in range(TILES):
                for k in range(2):
                    pool.indirect_dma_start(
                        out=slot_d, out_offset=bass.IndirectOffsetOnAxis(ap=slot[0:ROWS[t], k, t:t + 1], axis=0),
                        in_=tokid[0:ROWS[t], t:t + 1], in_offset=None).then_inc(slot_stored, 16)
            pool.wait_ge(slot_stored, 16 * 2 * TILES)
            pool.dma_start(idx_all[:, 0:ROUNDS * NE].rearrange("p (r e) -> p r e", r=ROUNDS),
                           slot_d.rearrange("(r p e) a -> p r (e a)", p=SLOTS, e=NE)).then_inc(idx_in, 16)
            pool.wait_ge(idx_in, 16)
            with pool.Fori(1, NE // 2 + 1) as p:
                gather(p * 2, 0)
                gather(p * 2 + 1, 1)
            most = pool.value_load(cnti[0:1, 0:1], min_val=0, max_val=NTOK)
            with pool.If(most > SLOTS):
                with pool.Fori(NE // 2 + 1, ROUNDS * NE // 2 + 1) as p:
                    gather(p * 2, 0)
                    gather(p * 2 + 1, 1)
                take_rows(y_d, ROUNDS * NE)
            with pool.Else():
                take_rows(y_d[0:SLOTS * NE, :], NE)
            for t in range(TILES):
                rsqrt(N_FINAL + t)
            pool.wait_ge(other_stored, 16 * stores[0])
            pool.wait_ge(v_stored, 64)
            pool.wait_ge(mk_stored, 32)
            for t in range(TILES):
                pool.wait_ge(ktok_stored[t], 32)

        @block.scalar
        def _(act):
            act.dma_start(gcol[:, 0, :], i["g_mix"][0].rearrange("(p c) -> p c", c=C)).then_inc(gmix_in, 16)

            def norm(n, parts, before=None):
                rows = unit_rows(n)
                dst = hn[0:rows, n % 2, :]
                if n >= 2:
                    act.wait_ge(t_ready, t_of[n - 2] + 2)
                for k, (src, lo, hi) in enumerate(parts):
                    last = act.activation(dst[:, lo:hi], src, ACT.Square, accum_out=ss[0:rows, 2 * n + k:2 * n + k + 1])
                last.then_inc(sq_done, 1)
                act.wait_ge(rstd_done, n + 1)
                for k, (src, lo, hi) in enumerate(parts):
                    last = act.activation(dst[:, lo:hi], src, ACT.Copy, scale=rstd[0:rows, 2 * n + k:2 * n + k + 1])
                last.then_inc(hn_ready, 1)

            def evacuate(j, dst, src, scale=1.0, last=True):
                act.wait_ge(a_ready, j + 1)
                ins = act.activation(dst, src, ACT.Copy, scale=scale)
                if last:
                    ins.then_inc(a_used, 1)

            for t in range(TILES):
                act.wait_ge(x_in[t], 16)
                norm(N_MIX + t, [(xres[0:ROWS[t], t, :], 0, D)])

            def softmax_unit(g, u, n):
                h, t, keys = units(g)[u]
                act.wait_ge(max_ready, n + 1)
                rows = srow_t[t][0:ROWS[t], 0:keys]
                act.activation(rows, rows, ACT.Exp, bias=negmax[0:ROWS[t], t:t + 1],
                               accum_out=rowsum[0:ROWS[t], t:t + 1]).then_inc(exp_done, 1)

            def output_unit(g, u, n, j):
                h, t, _ = units(g)[u]
                rows, dh = ROWS[t], (DH if g < 2 else 128)
                col = (W if g == 1 else 0) + h * dh
                act.wait_ge(rinv_done, n + 1)
                evacuate(j, oall[0:rows, t, col:col + dh], pA[j % 2][0:rows, 0:dh], rinv[0:rows, t:t + 1])

            def attention(g, n0, j0):
                k = len(units(g))
                for s in range(k + 3):
                    if s < k:
                        softmax_unit(g, s, n0 + s)
                    if s >= 3:
                        output_unit(g, s - 3, n0 + s - 3, j0 + s - 3)

            for g in range(2):
                j = A_GROUP[g]
                for m in range(M4):
                    evacuate(j + m, qT[:, m, :], pA[(j + m) % 2][:, 0:NTOK], Q_SCALE)
                for m in range(M4):
                    evacuate(j + 4 + m, kT[:, m, :], pA[(j + 4 + m) % 2][:, 0:NTOK])
                if g == 1:
                    act.wait_ge(v_stored, 32)
                for t in range(TILES):
                    evacuate(j + 8 + t, v[0:ROWS[t], t, :], pA[(j + 8 + t) % 2][0:ROWS[t], :])
                if g == 0:
                    act.wait_ge(consts, 2)
                    evacuate(A_FL, flx[:, 0:16], pA[A_FL % 2][:, 0:16], last=False)
                    evacuate(A_FL, flx[0:64, 16:24], pA[A_FL % 2][0:64, 16:24])
                    act.wait_ge(z_ready, 1)
                    act.activation(fla[:, :], fla[:, :], ACT.Exp).then_inc(act_step, 1)
                    act.wait_ge(act_step, 1)
                    act.activation(fla[:, :], fla[:, :], ACT.Ln, bias=1.0).then_inc(ln_ready, 1)
                    for x in range(4):
                        evacuate(A_REL + x, relb[:, 2 * x:2 * x + 2, :], pA[(A_REL + x) % 2][:, :].rearrange("p (h k) -> p h k", h=2))
                    evacuate(A_CTOK, cq[:, 0:16], pA[A_CTOK % 2][:, 0:16], last=False)
                    evacuate(A_CTOK, cq[0:64, 16:24], pA[A_CTOK % 2][0:64, 16:24])
                    for j, lo, hi, c0 in CK_PARTS:
                        act.wait_ge(a_ready, j + 1)
                        act.activation(ckT[:, lo:hi], pA[j % 2][:, c0:c0 + hi - lo], ACT.Copy, scale=-1.0).then_inc(ck_hi, 1)
                attention(g, 24 * g, A_PV[g])

            act.wait_ge(a_used, A_WOUT)
            for t in range(TILES):
                o_t = oall[0:ROWS[t], t, :]
                norm(N_MERGE + t, [(o_t[:, 0:W], 0, W), (o_t[:, W:], W, D)])
            act.wait_ge(xmem_in, 16)
            for t in range(MB):
                norm(N_MEM + t, [(xmem[:, t, :], 0, D)])

            def cross_norm(t):
                act.wait_ge(a_used, A_WOUT + 2 * t + 2)
                norm(N_CROSS + t, [(xres[0:ROWS[t], t, :], 0, D)])

            cross_norm(0)
            cross_norm(1)
            act.wait_ge(v_stored, 64)
            for m in range(HM):
                evacuate(A_MEM + m, mkT[:, m, :], pA[(A_MEM + m) % 2][:, 0:NMEM])
            cross_norm(2)
            for b in range(MB):
                evacuate(A_MEM + HM + b, mv[:, b, :], pA[(A_MEM + HM + b) % 2][:, :])
            for m in range(M4):
                evacuate(A_CQ + m, qxT[:, m, :], pA[(A_CQ + m) % 2][:, 0:NTOK])
            attention(2, 48, A_XPV)
            for t in range(TILES):
                if t == 2:
                    act.wait_ge(hn_stored[0], 16)
                act.wait_ge(a_used, A_CO + 2 * t + 2)
                norm(N_FFN + t, [(xres[0:ROWS[t], t, :], 0, D)])
            act.wait_ge(top1_ready, 1)
            for t in range(TILES):
                ins = act.activation(ex4[:, t, :], lg[:, t, 0:NG], ACT.Exp, bias=nm1[:, t:t + 1], accum_out=s4[:, t:t + 1])
            ins.then_inc(ex4_ready, 1)
            act.wait_ge(dlt_ready, 1)
            act.activation(edl[:, :], dlt[:, :], ACT.Exp).then_inc(edl_ready, 1)

            def split(b, chunks):
                for f in chunks:
                    act.activation(w_hi[:, f, :], by_k(3 * b + 2, FC)[:, f, :], ACT.Copy).then_inc(w_hi_ready, 1)

            def sigmoid(n, b, first=False):
                act.wait_ge(gu_ready, n + 1)
                if not first:
                    act.wait_ge(at_ready, n - 1)
                act.activation(sg[:, b, :], pA[b][:, 0:GW], ACT.Sigmoid).then_inc(sig_ready, 1)

            def lower_rows(n, b, first=False):
                act.wait_ge(y_ready, n + 1)
                if not first:
                    act.wait_ge(y_stored[b], (n - b) * 8)
                act.activation(ysb[:, b, :], pS[b][SLOTS:2 * SLOTS, :], ACT.Copy).then_inc(y_lower, 1)

            def rows_out(n, b, r, e):
                act.wait_ge(y_summed, n + 1)
                at_r = r if isinstance(r, int) else bass.ds(r, 1)
                at_e = e if isinstance(e, int) else bass.ds(e, 1)
                dst = y_d.rearrange("(r p e) d -> r e p d", p=SLOTS, e=NE)[at_r, at_e]
                if len(dst.shape) == 4:
                    dst = dst.rearrange("a b p d -> (a b p) d")
                elif len(dst.shape) == 3:
                    dst = dst.rearrange("a p d -> (a p) d")
                act.dma_start(dst, ysb[:, b, :]).then_inc(y_stored[b], 16)

            def expert(r, e, b, first=False, first_out=False):
                n = r * NE + e
                lower_rows(n - 1, 1 - b, first_out)
                act.wait_ge(w_in_s[3 * b + 2], (n - b) * 8 + 48)
                split(b, (0,))
                rows_out(n - 1, 1 - b, r, e - 1)
                split(b, range(1, FC))
                sigmoid(n, b, first)

            def experts(r):
                n = r * NE
                act.wait_ge(w_in_s[2], n * 8 + 48)
                split(0, range(FC))
                first = isinstance(r, int)
                sigmoid(n, 0, first)
                expert(r, 1, 1, first, first)
                expert(r, 2, 0, False, first)
                expert(r, 3, 1)
                with act.Fori(2, NE // 2) as p:
                    for b in range(2):
                        expert(r, p * 2 + b, b)
                n += NE - 1
                lower_rows(n, 1)
                rows_out(n, 1, r, NE - 1)

            act.wait_ge(a_ready, A_ROUTE + 1)
            for t in range(TILES):
                act.wait_ge(hn_stored[t], 16)
            experts(0)
            for b in range(2):
                act.wait_ge(y_stored[b], 16 * (NE // 2))
            most = act.value_load(cnti[0:1, 0:1], min_val=0, max_val=NTOK)
            with act.If(most > SLOTS):
                with act.Fori(1, ROUNDS) as r:
                    experts(r)
                for b in range(2):
                    act.wait_ge(y_stored[b], 16 * (ROUNDS * NE // 2))
            act.activation(sg[:, 0, 0:1], ones[:, 0:1], ACT.Copy).then_inc(moe_done, 1)
            for t in range(TILES):
                rows, n = ROWS[t], N_FINAL + t
                act.wait_ge(xfin_ready, t + 1)
                act.activation(oall[0:rows, t, :], xres[0:rows, t, :], ACT.Square,
                               accum_out=ss[0:rows, 2 * n:2 * n + 1]).then_inc(sq_done, 1)

        @block.tensor
        def _(pe):
            mm = nc.tensor.matmul

            def a_bank(j):
                if j >= 2:
                    pe.wait_ge(a_used, j - 1)
                return pA[j % 2]

            def t_bank(j):
                if j >= 2:
                    pe.wait_ge(t_used, j - 1)
                return pTr[j % 2]

            def weights(j):
                pe.wait_ge(w_in_s[j % RING], 16 * (j // RING + 1))
                return by_k(j, front_weights[j].shape[1])

            def transpose_norm(n, j, rows):
                pe.wait_ge(hn_ready, n + 1)
                src = hn[0:rows, n % 2, :].rearrange("t (p c) -> t c p", c=C)
                for half in range(2):
                    bank = t_bank(j + half)
                    for c in range(4):
                        last = nc.tensor.transpose(bank[:, c * P:c * P + rows], src[:, 4 * half + c, :], ident[0:rows, 0:rows])
                    if half == 0:
                        last.then_inc(t_ready, 1)
                last.then_inc(t_ready, 1)

            def by_weights(j, w, xT, n, m):
                bank = a_bank(j)
                for c in range(C):
                    last = mm(bank[:, 0:n], w[:, c, m * P:(m + 1) * P], xT[:, c, 0:n], start=c == 0, stop=c == C - 1)
                last.then_inc(a_ready, 1)
                return last

            def by_tokens(j, lhs, w, k, cols_, rows):
                bank = a_bank(j)
                for c in range(k):
                    last = mm(bank[0:rows, 0:512], lhs(c), w[:, c, cols_], start=c == 0, stop=c == k - 1)
                last.then_inc(a_ready, 1)

            pe.wait_ge(consts, 1)
            for t in range(TILES):
                transpose_norm(N_MIX + t, T_MIX + 2 * t, ROWS[t])
            pe.wait_ge(t_used, T_CACHE[0])

            def attention(g, n0, j0, t0):
                us = units(g)
                tj = [t0]
                ready_at = {}

                def scores(u):
                    h, t, keys = us[u]
                    n = n0 + u
                    rows, q0 = ROWS[t], OFF[t]
                    if n >= 3:
                        pe.wait_ge(sc_used, n - 2)
                    bank = score_banks[t]
                    if g == 2:
                        kk = mkT if t < 2 else cmkT
                        mm(bank[0:rows, 0:keys], qxT[:, h, q0:q0 + rows], kk[:, h, :], start=True, stop=True).then_inc(sc_ready, 1)
                        return
                    p0, m = 64 * (h % 2), h // 2
                    ps = slice(p0, p0 + DH)
                    q = qT[ps, m, q0:q0 + rows]
                    if t < 2:
                        segs = [(0, keys, kT[ps, m, 0:keys], ckT[p0:p0 + 40, 0:keys])]
                    else:
                        segs = [(0, PAST, kcT[ps, m, :], ckT[p0:p0 + 40, NP_TOK:own]),
                                (PAST, keys, kT[ps, m, NP_TOK:NTOK], ckT[p0:p0 + 40, own:own + NS_TOK])]
                    for lo, hi, k, c in segs:
                        last = mm(bank[0:rows, lo:hi], q, k, start=True, stop=g == 1)
                        if g == 0:
                            of_h = selr[p0:p0 + 40, h:h + 1].to_broadcast([40, rows])
                            last = mm(bank[0:rows, lo:hi], of_h, c, start=False, stop=True)
                    last.then_inc(sc_ready, 1)

                def turn(u):
                    h, t, keys = us[u]
                    n, rows = n0 + u, ROWS[t]
                    pe.wait_ge(exp_done, n + 1)
                    blocks = [(k, min(P, keys - k)) for k in range(0, keys, P)]
                    for g0 in range(0, len(blocks), 4):
                        bank = t_bank(tj[0])
                        for x, (k, w) in enumerate(blocks[g0:g0 + 4]):
                            last = nc.tensor.transpose(bank[0:w, x * P:x * P + rows], srow_t[t][0:rows, k:k + w], ident[0:rows, 0:rows])
                        last.then_inc(t_ready, 1)
                        tj[0] += 1
                    ready_at[u] = tj[0]

                def values(u):
                    h, t, keys = us[u]
                    n, rows = n0 + u, ROWS[t]
                    pe.wait_ge(t_used, ready_at[u])
                    bank = a_bank(j0 + u)
                    nb = -(-keys // P)
                    for b in range(nb):
                        w = min(P, keys - b * P)
                        if g == 2:
                            src = (mv if t < 2 else cmv)[:, b, h * P:(h + 1) * P]
                        elif t == 2 and b < PB:
                            src = vc[:, b, h * DH:(h + 1) * DH]
                        else:
                            src = v[0:w, b if t < 2 else 2, h * DH:(h + 1) * DH]
                        last = mm(bank[0:rows, 0:P if g == 2 else DH], pT_t[t][0:w, b, 0:rows], src, start=b == 0, stop=b == nb - 1)
                    last.then_inc(a_ready, 1)

                for s in range(len(us) + 3):
                    if s < len(us):
                        scores(s)
                    if 2 <= s < len(us) + 2:
                        turn(s - 2)
                    if s >= 3:
                        values(s - 3)

            for g in range(2):
                j = A_GROUP[g]
                w = weights(J_Q + 3 * g)
                for m in range(M4):
                    by_weights(j + m, w, hT, NTOK, m)
                w = weights(J_K + 3 * g)
                for m in range(M4):
                    by_weights(j + 4 + m, w, hT, NTOK, m)
                w = weights(J_V + 3 * g)
                for t in range(TILES):
                    by_tokens(j + 8 + t, lambda c: hT[:, c, OFF[t]:OFF[t] + ROWS[t]], w, C, slice(0, 512), ROWS[t])
                if g == 0:
                    pe.wait_ge(small_in, SMALL)
                    bank = a_bank(A_FL)
                    for t in range(TILES):
                        for c in range(C):
                            last = mm(bank[0:ROWS[t], 8 * t:8 * t + 8], hT[:, c, OFF[t]:OFF[t] + ROWS[t]], wfl[:, c, :],
                                      start=c == 0, stop=c == C - 1)
                    last.then_inc(a_ready, 1)
                pe.wait_ge(stage_in[g], 16)
                for b in range(PB):
                    bank = t_bank(T_CACHE[g] + b)
                    for m in range(M4):
                        last = nc.tensor.transpose(bank[:, m * P:(m + 1) * P], stage[:, b, m * P:(m + 1) * P], ident[:, :])
                    last.then_inc(t_ready, 1)
                pe.wait_ge(a_used, j + 8)
                for t in range(TILES):
                    bank = t_bank(T_KBACK[g] + t)
                    for m in range(M4):
                        last = nc.tensor.transpose(bank[0:ROWS[t], m * P:(m + 1) * P], kT[:, m, OFF[t]:OFF[t] + ROWS[t]], ident[:, :])
                    last.then_inc(t_ready, 1)
                if g == 0:
                    pe.wait_ge(rel_in, 16)
                    for x in range(4):
                        bank = a_bank(A_REL + x)
                        for h in (2 * x, 2 * x + 1):
                            for kb in range(2):
                                c0 = 256 * (h % 2) + P * kb
                                last = mm(bank[:, c0:c0 + P], hankel[:, h, P * (1 - kb):P * (2 - kb)], anti[:, :], start=True, stop=True)
                        last.then_inc(a_ready, 1)
                    pe.wait_ge(lfpad_ready, 1)

                    def cumulate(bank, c0, blocks, rows, heads_first):
                        for x, (lf, k) in enumerate(blocks):
                            last_one = x == len(blocks) - 1
                            m_ = (tri if last_one else ones)[0:k, 0:rows]
                            if heads_first:
                                r = mm(bank[:, c0:c0 + rows], lf, m_, start=x == 0, stop=last_one)
                            else:
                                r = mm(bank[0:rows, c0:c0 + 8], m_, lf[:, 0:HEADS], start=x == 0, stop=last_one)
                        return r

                    prompt = [(lfpad[:, 0, :], P), (lfpad[:, 1, :], P)]
                    past = [(clfpad[:, b, :], P) for b in range(PB)]
                    sample = past + [(lfpad[0:NS_TOK, 2, :], NS_TOK)]
                    bank = a_bank(A_CTOK)
                    cumulate(bank, 0, prompt[:1], P, False)
                    cumulate(bank, 8, prompt, P, False)
                    cumulate(bank, 16, sample, NS_TOK, False).then_inc(a_ready, 1)
                    bank = a_bank(A_CPRO)
                    cumulate(bank, 0, prompt[:1], P, True)
                    cumulate(bank, P, prompt, P, True)
                    cumulate(bank, NP_TOK, sample, NS_TOK, True).then_inc(a_ready, 1)
                    bank = a_bank(A_CPAST)
                    for b in range(PB):
                        last = cumulate(bank, b * P, past[:b + 1], P, True)
                    last.then_inc(a_ready, 1)
                    pe.wait_ge(consts, 3)
                pe.wait_ge(a_used, A_PV[g])
                pe.wait_ge(t_used, T_ATT[g])
                pe.wait_ge(vc_in[g], 16)
                attention(g, 24 * g, A_PV[g], T_ATT[g])

            def merge_turn(t):
                transpose_norm(N_MERGE + t, T_MERGE + 2 * t, ROWS[t])

            def merge_out(t, half):
                pe.wait_ge(t_used, T_MERGE + 2 * t + 2)
                by_tokens(A_WOUT + 2 * t + half, lambda c: hT[:, c, OFF[t]:OFF[t] + ROWS[t]], w2[half], C, slice(0, 512), ROWS[t])

            merge_turn(0)
            w2 = [weights(J_WOUT), weights(J_WOUT + 1)]
            merge_out(0, 0)
            merge_turn(1)
            merge_out(0, 1)
            merge_out(1, 0)
            merge_turn(2)
            merge_out(1, 1)
            merge_out(2, 0)
            merge_out(2, 1)
            for t in range(MB):
                transpose_norm(N_MEM + t, T_MEM + 2 * t, P)
            pe.wait_ge(cmk_in, 16)
            for b in range(MB):
                bank = t_bank(T_CMK + b)
                for m in range(M4):
                    last = nc.tensor.transpose(bank[:, m * P:(m + 1) * P], ktok[:, b, m * P:(m + 1) * P], ident[:, :])
                last.then_inc(t_ready, 1)
            transpose_norm(N_CROSS, T_CROSS, ROWS[0])
            transpose_norm(N_CROSS + 1, T_CROSS + 2, ROWS[1])
            w = weights(J_CK)
            for m in range(HM):
                by_weights(A_MEM + m, w, memT, NMEM, m)
            w = weights(J_CV)
            for b in range(MB):
                if b == 1:
                    transpose_norm(N_CROSS + 2, T_CROSS + 4, ROWS[2])
                by_tokens(A_MEM + HM + b, lambda c: memT[:, c, b * P:(b + 1) * P], w, C, slice(0, 512), P)
            pe.wait_ge(a_used, A_MEM + HM)
            for b in range(MB):
                bank = t_bank(T_MKBACK + b)
                for m in range(HM):
                    last = nc.tensor.transpose(bank[:, m * P:(m + 1) * P], mkT[:, m, b * P:(b + 1) * P], ident[:, :])
                last.then_inc(t_ready, 1)
            pe.wait_ge(t_used, T_CROSS + 6)
            w = weights(J_CQ)
            for m in range(M4):
                by_weights(A_CQ + m, w, hT, NTOK, m)
            pe.wait_ge(a_used, A_XPV)
            pe.wait_ge(cmv_in, 16)
            attention(2, 48, A_XPV, T_XATT)
            pe.wait_ge(a_used, A_CO)
            for t in range(TILES):
                bank = t_bank(T_OX + t)
                for m in range(M4):
                    last = nc.tensor.transpose(bank[:, m * P:m * P + ROWS[t]], oall[0:ROWS[t], t, m * P:(m + 1) * P], ident[0:ROWS[t], 0:ROWS[t]])
                last.then_inc(t_ready, 1)
            pe.wait_ge(t_used, T_FFN)
            w = weights(J_CO)
            R = NG + NE

            def out_tile(t):
                for half in range(2):
                    by_tokens(A_CO + 2 * t + half, lambda c: hT[:, c, OFF[t]:OFF[t] + ROWS[t]], w, M4, slice(half * 512, half * 512 + 512), ROWS[t])

            def route_tile(t):
                pe.wait_ge(t_used, T_FFN + 2 * t + 2)
                for c in range(C):
                    last = mm(bank[0:ROWS[t], R * t:R * t + R], hT[:, c, OFF[t]:OFF[t] + ROWS[t]], wr[:, c, :], start=c == 0, stop=c == C - 1)
                return last

            out_tile(0)
            out_tile(1)
            transpose_norm(N_FFN, T_FFN, ROWS[0])
            out_tile(2)
            transpose_norm(N_FFN + 1, T_FFN + 2, ROWS[1])
            bank = a_bank(A_ROUTE)
            route_tile(0)
            route_tile(1)
            transpose_norm(N_FFN + 2, T_FFN + 4, ROWS[2])
            route_tile(2).then_inc(a_ready, 1)
            pe.wait_ge(moh_ready, 1)
            bank = a_bank(A_POS)
            for t in range(TILES):
                for x in range(t + 1):
                    last_one = x == t
                    mm(bank[0:ROWS[t], NE * t:NE * t + NE], (stri if last_one else ones)[0:ROWS[x], 0:ROWS[t]],
                       mboth[0:ROWS[x], x, :], start=x == 0, stop=last_one)
            for t in range(TILES):
                last = mm(bank[:, NE * TILES:NE * (TILES + 1)], ones[0:ROWS[t], :], mboth[0:ROWS[t], t, :], start=t == 0, stop=t == 2)
            last.then_inc(a_ready, 1)
            pe.wait_ge(in_place_ready, 1)
            bank = a_bank(A_LIST)
            for e in range(2):
                for t in range(TILES):
                    last = mm(bank[0:SLOTS, e:e + 1], in_place[0:ROWS[t], t, e, :], tokf[0:ROWS[t], t:t + 1], start=t == 0, stop=t == TILES - 1)
            last.then_inc(a_ready, 1)
            pe.wait_ge(a_used, A_LIST + 1)

            def transpose_rows(n, b):
                pe.wait_ge(xg_in[b], (n - b) * 8 + 16)
                pe.nop().then_inc(pe_passed, 1)
                src = xg[:, b, :].rearrange("s (p c) -> s c p", c=C)
                for c in range(C):
                    last = nc.tensor.transpose(pTr[b][:, c * SLOTS:(c + 1) * SLOTS], src[:, c, :], ident[0:SLOTS, 0:SLOTS])
                last.then_inc(xt_ready, 1)

            def keep_warm(bank, count, width=512):
                for _ in range(count):
                    mm(bank[:, 0:width], ident[:, :], xres[:, 0, 0:width], start=True, stop=True)

            def product(n, b, x):
                pe.wait_ge(w_in_s[3 * b + x], (n - b) * 8 + 48)
                w = by_k(3 * b + x)
                for f in range(FC):
                    for c in range(C):
                        last = mm(pA[b][:, x * GW + f * SLOTS:x * GW + (f + 1) * SLOTS], w[:, c, f * P:(f + 1) * P],
                                  xeT[:, b, c, :], start=c == 0, stop=c == C - 1)
                last.then_inc(gu_ready if x else gate_read, 1)

            def down(n, b, first=False):
                pe.wait_ge(at_ready, n + 1)
                if not first:
                    pe.wait_ge(y_summed, n - 1)
                for f in range(FC):
                    a = a_split[:, b, f, :, :].rearrange("p k s -> p (k s)")
                    pe.wait_ge(w_lo_ready, n * FC + f + 1)
                    for half in range(2):
                        for part in (w_hi, w_lo):
                            last = mm(pS[b][0:2 * SLOTS, half * 512:(half + 1) * 512], a, part[:, f, half * 512:(half + 1) * 512],
                                      start=f == 0 and part is w_hi, stop=f == FC - 1 and part is w_lo)
                last.then_inc(y_ready, 1)

            def experts(r):
                n = r * NE
                first = isinstance(r, int)

                def expert(n, b, first=False):
                    if not first:
                        keep_warm(pA[b], 1, 256)
                    pe.wait_ge(xe_ready, n + 1)
                    product(n, b, 0)
                    down(n - 1, 1 - b, first)
                    product(n, b, 1)
                    transpose_rows(n + 2, b)

                pe.wait_ge(xe_ready, n + 1)
                product(n, 0, 0)
                product(n, 0, 1)
                transpose_rows(n + 2, 0)
                for e in range(1, 4):
                    expert(n + e, e % 2, first and e < 3)
                with pe.Fori(2, NE // 2) as p:
                    for b in range(2):
                        expert(n + p * 2 + b, b)
                keep_warm(pA[0], 3)
                down(n + NE - 1, 1)

            keep_warm(pS[0], 6)
            transpose_rows(0, 0)
            transpose_rows(1, 1)
            keep_warm(pS[0], 1)
            experts(0)
            most = pe.value_load(cnti[0:1, 0:1], min_val=0, max_val=NTOK)
            with pe.If(most > SLOTS):
                with pe.Fori(1, ROUNDS) as r:
                    experts(r)

        @block.vector
        def _(dve):
            nv = nc.vector
            steps = [0]

            def step(ins):
                steps[0] += 1
                ins.then_inc(dve_step, 1)
                dve.wait_ge(dve_step, steps[0])

            nv.memset(flx[:, :], 0.0)
            nv.memset(lg[:, :, :], 0.0)
            nv.memset(posb[:, :, :], 0.0)
            nv.memset(lfpad, 0.0)
            nv.memset(clfpad, 0.0)
            nv.memset(lg8[:, :, :], -3e38).then_inc(consts, 1)
            dve.wait_ge(consts, 2)
            nv.tensor_tensor(fla[:, 0:8], ident[:, 0:8], ident[:, 32:40], ALU.add)
            step(nv.tensor_tensor(fla[:, 8:16], ident[:, 64:72], ident[:, 96:104], ALU.add))
            nv.tensor_tensor(selr[:, :], fla[:, 0:8], fla[:, 8:16], ALU.add).then_inc(consts, 1)
            dve.wait_ge(gmix_in, 16)

            def norm(j, rows, dstT, off, gain):
                for half in range(2):
                    dve.wait_ge(t_ready, j + half + 1)
                    src = pTr[(j + half) % 2][:, :].rearrange("p (c t) -> p c t", c=4)[:, :, 0:rows]
                    gg = gcol[:, gain, 4 * half:4 * half + 4].unsqueeze(2).to_broadcast([P, 4, rows])
                    nv.tensor_tensor(dstT[:, 4 * half:4 * half + 4, off:off + rows], src, gg, ALU.mult).then_inc(t_used, 1)

            for t in range(TILES):
                norm(T_MIX + 2 * t, ROWS[t], hT, OFF[t], 0)
            dve.wait_ge(rel_raw, 16)
            nv.tensor_copy(relT[:, 2 * CLIP + 1:384], relT[:, 2 * CLIP:2 * CLIP + 1].to_broadcast([HEADS, 127])).then_inc(rel_rows, 1)
            dve.wait_ge(small_in, SMALL)

            def attention(g, n0, j0, t0):
                us = units(g)
                tj = [t0]

                def scores(u):
                    h, t, keys = us[u]
                    n, rows = n0 + u, ROWS[t]
                    dst, bank = srow_t[t][0:rows], score_banks[t][0:rows]
                    dve.wait_ge(sc_ready, n + 1)
                    if g == 0:
                        c = cq[0:rows, 8 * t + h:8 * t + h + 1]
                        if t == 2:
                            nv.tensor_scalar(dst[:, 0:PAST], bank[:, 0:PAST], c, None, ALU.add)
                            lo, mask = PAST, cmask[0:rows, P:P + NS_TOK]
                        else:
                            lo, mask = 0, cmask[:, 256 - keys:256]
                        ins = nv.scalar_tensor_tensor(dst[:, lo:keys], bank[:, lo:keys], c, mask, ALU.add, ALU.add)
                    elif g == 1:
                        if t == 2:
                            far = PAST - P
                            nv.tensor_scalar(dst[:, 0:far], bank[:, 0:far], t256[:, h:h + 1], None, ALU.add)
                            lo, bias = far, relb[0:rows, h, 0:keys - far]
                        else:
                            lo, bias = 0, relb[:, h, 256 - keys:256]
                        ins = nv.tensor_tensor(dst[:, lo:keys], bank[:, lo:keys], bias, ALU.add)
                    else:
                        ins = nv.tensor_scalar(dst[:, 0:keys], bank[:, 0:keys], MEM_SCALE, None, ALU.mult)
                    ins.then_inc(sc_used, 1)
                    dve.wait_ge(sc_used, n + 1)
                    nv.reduce_max(negmax[0:rows, t:t + 1], dst[:, 0:keys], AX.X, negate=True).then_inc(max_ready, 1)

                def turned(u):
                    h, t, keys = us[u]
                    n, rows = n0 + u, ROWS[t]
                    dve.wait_ge(exp_done, n + 1)
                    if u >= 3:
                        dve.wait_ge(a_used, j0 + u - 2)
                    nv.reciprocal(rinv[0:rows, t:t + 1], rowsum[0:rows, t:t + 1]).then_inc(rinv_done, 1)
                    nb = -(-keys // P)
                    for b0 in range(0, nb, 4):
                        k = min(4, nb - b0)
                        w = min(P, keys - b0 * P)
                        dve.wait_ge(t_ready, tj[0] + 1)
                        src = pTr[tj[0] % 2][0:w, 0:k * P].rearrange("p (b q) -> p b q", q=P)[:, :, 0:rows]
                        nv.tensor_copy(pT_t[t][0:w, b0:b0 + k, 0:rows], src).then_inc(t_used, 1)
                        tj[0] += 1

                for s in range(len(us) + 2):
                    if s < len(us):
                        scores(s)
                    if s >= 2:
                        turned(s - 2)

            def to_cols(j, dst, rows=P, width=512):
                dve.wait_ge(t_ready, j + 1)
                nv.tensor_copy(dst, pTr[j % 2][0:rows, 0:width].rearrange("p (m k) -> p m k", m=4)).then_inc(t_used, 1)

            for g in range(2):
                if g == 0:
                    dve.wait_ge(a_used, A_FL + 1)
                    step(nv.tensor_tensor(flz[:, :].rearrange("p (t h) -> p t h", t=TILES), flx[:, :].rearrange("p (t h) -> p t h", t=TILES),
                                          bfb[:, :].unsqueeze(1).to_broadcast([P, TILES, HEADS]), ALU.add))
                    nv.scalar_tensor_tensor(fla[:, :], flz[:, :], -1.0, flz[:, :], ALU.mult, ALU.min).then_inc(z_ready, 1)
                for b in range(PB):
                    to_cols(T_CACHE[g] + b, kcT[:, :, b * P:(b + 1) * P])
                for t in range(TILES):
                    if g == 1:
                        dve.wait_ge(ktok_stored[t], 16)
                    dve.wait_ge(t_ready, T_KBACK[g] + t + 1)
                    nv.tensor_copy(ktok[0:ROWS[t], t, :], pTr[(T_KBACK[g] + t) % 2][0:ROWS[t], :]).then_inc(t_used, 1)
                if g == 0:
                    dve.wait_ge(ln_ready, 1)
                    nv.scalar_tensor_tensor(lfb[:, :, :].rearrange("p t h -> p (t h)"), flz[:, :], 0.0, fla[:, :], ALU.min, ALU.subtract).then_inc(lf_ready, 1)
                    dve.wait_ge(lf_ready, 1)
                    for n, pad, lf in ((PB, clfpad, clf), (TILES, lfpad, lfb)):
                        ins = nv.tensor_copy(pad.rearrange("p b (four w) -> p b four w", four=4)[:, :, :, 0:HEADS],
                                             lf[:, :, :].unsqueeze(2).to_broadcast([P, n, 4, HEADS]))
                    ins.then_inc(lfpad_ready, 1)
                    dve.wait_ge(a_used, A_CTOK + 1)
                    for x, (j, lo, hi, c0) in enumerate(CK_PARTS):
                        dve.wait_ge(ck_hi, max(x + 1, 2))
                        for p0 in (32, 96):
                            ps = slice(p0, p0 + 32)
                            ins = nv.scalar_tensor_tensor(ckT[ps, lo:hi], pA[j % 2][ps, c0:c0 + hi - lo], -1.0,
                                                          ckT[ps, lo:hi].bitcast(F32), ALU.mult, ALU.subtract)
                        if x > 0:
                            ins.then_inc(a_used, 1)
                    dve.wait_ge(rel_in, 16)
                else:
                    dve.wait_ge(rel_ready, 1)
                attention(g, 24 * g, A_PV[g], T_ATT[g])

            def residual(j, t, half):
                rows = ROWS[t]
                dve.wait_ge(a_ready, j + 1)
                x = xres[0:rows, t, half * 512:(half + 1) * 512]
                nv.tensor_tensor(x, x, pA[j % 2][0:rows, :], ALU.add).then_inc(a_used, 1)

            def merge_norm(t):
                norm(T_MERGE + 2 * t, ROWS[t], hT, OFF[t], 1)

            merge_norm(0)
            residual(A_WOUT, 0, 0)
            merge_norm(1)
            residual(A_WOUT + 1, 0, 1)
            residual(A_WOUT + 2, 1, 0)
            merge_norm(2)
            residual(A_WOUT + 3, 1, 1)
            residual(A_WOUT + 4, 2, 0)
            residual(A_WOUT + 5, 2, 1)
            for t in range(MB):
                norm(T_MEM + 2 * t, P, memT, t * P, 2)
            for b in range(MB):
                to_cols(T_CMK + b, cmkT[:, :, b * P:(b + 1) * P])
            for t in range(TILES):
                norm(T_CROSS + 2 * t, ROWS[t], hT, OFF[t], 3)
            for b in range(MB):
                dve.wait_ge(t_ready, T_MKBACK + b + 1)
                nv.tensor_copy(mktok[:, b, :], pTr[(T_MKBACK + b) % 2][:, :]).then_inc(t_used, 1)
            attention(2, 48, A_XPV, T_XATT)
            for t in range(TILES):
                dve.wait_ge(t_ready, T_OX + t + 1)
                nv.tensor_copy(hT[:, 0:4, OFF[t]:OFF[t] + ROWS[t]],
                               pTr[(T_OX + t) % 2][:, :].rearrange("p (c t) -> p c t", c=4)[:, :, 0:ROWS[t]]).then_inc(t_used, 1)
            for t in range(TILES):
                for half in range(2):
                    residual(A_CO + 2 * t + half, t, half)
                if t >= 1:
                    norm(T_FFN + 2 * t - 2, ROWS[t - 1], hT, OFF[t - 1], 4)
            norm(T_FFN + 4, ROWS[2], hT, OFF[2], 4)

            R = NG + NE
            dve.wait_ge(a_ready, A_ROUTE + 1)
            nv.tensor_tensor(lg[:, 0:2, :], pA[A_ROUTE % 2][:, 0:2 * R].rearrange("p (t r) -> p t r", t=2),
                             brb[:, :].unsqueeze(1).to_broadcast([P, 2, R]), ALU.add)
            nv.tensor_tensor(lg[0:64, 2, :], pA[A_ROUTE % 2][0:64, 2 * R:3 * R], brb[0:64, :], ALU.add).then_inc(a_used, 1)
            dve.wait_ge(a_used, A_ROUTE + 1)
            step(nv.tensor_copy(lg8[:, :, 0:NG], lg[:, :, 0:NG]))
            for t in range(TILES):
                ins = nv.max(top1[:, t, :], lg8[:, t, :])
            step(ins)
            nv.tensor_scalar(nm1[:, :], top1[:, :, 0], -1.0, None, ALU.mult).then_inc(top1_ready, 1)
            for t in range(TILES):
                ins = nv.max_index(top1i[:, t, :], top1[:, t, :], lg8[:, t, :])
            step(ins)
            step(nv.tensor_copy(gidx[:, :], top1i[:, :, 0]))
            step(nv.tensor_tensor(goh[:, :, :], iota32[:, 0:NG].unsqueeze(1).to_broadcast([P, TILES, NG]),
                                  gidx[:, :].unsqueeze(2).to_broadcast([P, TILES, NG]), ALU.is_equal))
            for t in range(TILES):
                ins = nv.tensor_tensor(l2m[:, t, :, :], lg[:, t, NG:].rearrange("p (g e) -> p g e", g=NG),
                                       goh[:, t, :].unsqueeze(2).to_broadcast([P, NG, EPG]), ALU.mult)
            step(ins)
            step(nv.reduce_sum(l2g[:, :, :], l2m[:, :, :, :].rearrange("p t g e -> p t e g"), AX.X))
            for t in range(TILES):
                ins = nv.max(top2[:, t, :], l2g[:, t, :])
            step(ins)
            nv.tensor_tensor(dlt[:, :], top2[:, :, 1], top2[:, :, 0], ALU.subtract).then_inc(dlt_ready, 1)
            for t in range(TILES):
                ins = nv.max_index(top2i[:, t, :], top2[:, t, :], l2g[:, t, :])
            step(ins)
            for k in range(2):
                ins = nv.tensor_copy(eid[:, k, :], top2i[:, :, k])
            step(ins)
            for k in range(2):
                ins = nv.scalar_tensor_tensor(eid[:, k, :], gidx[:, :], float(EPG), eid[:, k, :], ALU.mult, ALU.add)
            step(ins)
            for k in range(2):
                ins = nv.tensor_tensor(moh[:, k, :, :], iota32[:, :].unsqueeze(1).to_broadcast([P, TILES, NE]),
                                       eid[:, k, :].unsqueeze(2).to_broadcast([P, TILES, NE]), ALU.is_equal)
            step(ins)
            nv.tensor_tensor(mboth[:, :, :], moh[:, 0, :, :], moh[:, 1, :, :], ALU.add).then_inc(moh_ready, 1)
            dve.wait_ge(ex4_ready, 1)
            step(nv.reciprocal(s4[:, :], s4[:, :]))
            dve.wait_ge(edl_ready, 1)
            step(nv.tensor_scalar(gate[:, 0, :], edl[:, :], 1.0, None, ALU.add))
            step(nv.reciprocal(gate[:, 0, :], gate[:, 0, :]))
            step(nv.tensor_tensor(gate[:, 0, :], gate[:, 0, :], s4[:, :], ALU.mult))
            step(nv.tensor_tensor(gate[:, 1, :], gate[:, 0, :], edl[:, :], ALU.mult))
            dve.wait_ge(a_ready, A_POS + 1)
            bank = pA[A_POS % 2]
            nv.tensor_copy(posb[:, 0:2, :], bank[:, 0:2 * NE].rearrange("p (t e) -> p t e", t=2))
            nv.tensor_copy(posb[0:64, 2, :], bank[0:64, 2 * NE:3 * NE])
            nv.reduce_max(cnt[:, 0:1], bank[:, 3 * NE:4 * NE], AX.X).then_inc(a_used, 1)
            dve.wait_ge(a_used, A_POS + 1)
            nv.scalar_tensor_tensor(place2[:, :, :], posb[:, :, 0:2], 1.0, mboth[:, :, 0:2], ALU.add, ALU.mult).then_inc(place2_ready, 1)
            dve.wait_ge(place2_ready, 1)
            for t in range(TILES):
                for e in range(2):
                    ins = nv.tensor_scalar(in_place[:, t, e, :], iota_slot[:, :], place2[:, t, e:e + 1], None, ALU.is_equal)
            ins.then_inc(in_place_ready, 1)
            dve.wait_ge(a_ready, A_LIST + 1)
            for e in range(2):
                ins = nv.tensor_copy(idx_cur[e][:, :], pA[A_LIST % 2][0:SLOTS, e:e + 1])
            ins.then_inc(a_used, 1)
            nv.tensor_copy(cnti[:, :], cnt[:, 0:1])
            for t in range(TILES):
                ins = nv.scalar_tensor_tensor(keyb[:, t, :], posb[:, t, :], float(NE), iota32[:, :], ALU.mult, ALU.add)
            step(ins)
            for k in range(2):
                step(nv.tensor_tensor(kprod[:, :, :], keyb[:, :, :], moh[:, k, :, :], ALU.mult))
                step(nv.reduce_sum(keyf[:, k, :], kprod[:, :, :], AX.X))
            nv.tensor_copy(slot[:, :, :], keyf[:, :, :]).then_inc(slot_ready, 1)

            def rows_in(n, b):
                dve.wait_ge(xt_ready, n + 1)
                nv.tensor_tensor(xeT[:, b, :, :], pTr[b][:, 0:C * SLOTS].rearrange("p (c s) -> p c s", c=C),
                                 gcol[:, 4, :].unsqueeze(2).to_broadcast([P, C, SLOTS]), ALU.mult).then_inc(xe_ready, 1)

            def activations(n, b, first=False):
                dve.wait_ge(sig_ready, n + 1)
                nv.tensor_tensor(sg[:, b, :], sg[:, b, :], pA[b][:, 0:GW], ALU.mult).then_inc(a_split_step, 1)
                dve.wait_ge(a_split_step, n * 3 + 1)
                nv.tensor_tensor(aT[:, b, :], sg[:, b, :], pA[b][:, GW:2 * GW], ALU.mult).then_inc(a_split_step, 1)
                dve.wait_ge(a_split_step, n * 3 + 2)
                if not first:
                    dve.wait_ge(y_ready, n - 1)
                a = aT[:, b, :].rearrange("p (f s) -> p f s", f=FC)
                nv.tensor_copy(a_split[:, b, :, 0, :], a).then_inc(a_split_step, 1)
                dve.wait_ge(a_split_step, n * 3 + 3)
                nv.tensor_tensor(a_split[:, b, :, 1, :], a, a_split[:, b, :, 0, :].bitcast(F32), ALU.subtract).then_inc(at_ready, 1)
                rows_in(n + 2, b)

            def lower_weights(n, b):
                for f in range(FC):
                    dve.wait_ge(w_hi_ready, n * FC + f + 1)
                    nv.tensor_tensor(w_lo[:, f, :], by_k(3 * b + 2, FC)[:, f, :], w_hi[:, f, :].bitcast(F32), ALU.subtract).then_inc(w_lo_ready, 1)

            def sum_rows(n, b):
                dve.wait_ge(y_lower, n + 1)
                nv.tensor_tensor(ysb[:, b, :], ysb[:, b, :], pS[b][0:SLOTS, :], ALU.add).then_inc(y_summed, 1)

            def expert(n, b, first=False):
                sum_rows(n - 1, 1 - b)
                lower_weights(n, b)
                activations(n, b, first)

            def experts(r):
                n = r * NE
                first = isinstance(r, int)
                lower_weights(n, 0)
                if first:
                    rows_in(0, 0)
                    rows_in(1, 1)
                activations(n, 0, first)
                expert(n + 1, 1, first)
                with dve.Fori(1, NE // 2) as p:
                    for b in range(2):
                        expert(n + p * 2 + b, b)
                sum_rows(n + NE - 1, 1)

            experts(0)
            most = dve.value_load(cnti[0:1, 0:1], min_val=0, max_val=NTOK)
            with dve.If(most > SLOTS):
                with dve.Fori(1, ROUNDS) as r:
                    experts(r)

            def sum_tile(t):
                rows = ROWS[t]
                dve.wait_ge(yg_in[t], 32)
                y0, y1, x = ygat[0:rows, t, 0, :], ygat[0:rows, t, 1, :], xres[0:rows, t, :]
                step(nv.scalar_tensor_tensor(x, y0, gate[0:rows, 0, t:t + 1], x, ALU.mult, ALU.add))
                nv.scalar_tensor_tensor(x, y1, gate[0:rows, 1, t:t + 1], x, ALU.mult, ALU.add).then_inc(xfin_ready, 1)

            def final(t):
                rows, n = ROWS[t], N_FINAL + t
                dve.wait_ge(rstd_done, n + 1)
                nv.scalar_tensor_tensor(oall[0:rows, t, :], xres[0:rows, t, :], rstd[0:rows, 2 * n:2 * n + 1], gfin[0:rows, :], ALU.mult, ALU.mult).then_inc(yout_ready, 1)

            dve.wait_ge(gfin_in, 16)
            sum_tile(0)
            sum_tile(1)
            final(0)
            sum_tile(2)
            final(1)
            final(2)


SMALL = 13 * 16


def unit_rows(n):
    if N_MEM <= n < N_CROSS:
        return P
    return ROWS[(n if n < N_MEM else n - N_CROSS) % 3]


_INS = ["x_prompt", "x_sample", "cache_fox_k", "cache_fox_v", "cache_fox_logf", "cache_band_k", "cache_band_v",
        "cache_mem_k", "cache_mem_v", "mem_prompt", "g_mix", "w_in", "b_forget", "g_out_fox", "g_out_band", "rel_table",
        "w_out", "g_cross", "g_mem", "w_cq", "w_ck", "w_cv", "w_co", "g_ffn", "w_router1", "b_router1", "w_router2",
        "b_router2", "w_exp_gate", "w_exp_up", "w_exp_down", "g_final"]
_OUTS = [("y_prompt", (1, 256, 1024)), ("y_sample", (1, 64, 1024)),
         ("fox_k_p", (1, 1, 256, 8, 64)), ("fox_v_p", (1, 1, 256, 8, 64)), ("fox_logf_p", (1, 1, 256, 8)),
         ("band_k_p", (1, 1, 256, 8, 64)), ("band_v_p", (1, 1, 256, 8, 64)),
         ("mem_k_p", (1, 1, 256, 4, 128)), ("mem_v_p", (1, 1, 256, 4, 128)),
         ("fox_k_s", (1, 1, 64, 8, 64)), ("fox_v_s", (1, 1, 64, 8, 64)), ("fox_logf_s", (1, 1, 64, 8)),
         ("band_k_s", (1, 1, 512, 8, 64)), ("band_v_s", (1, 1, 512, 8, 64))]


def kernel(**inputs):
    import numpy as np
    import concourse.bacc as bacc
    from concourse.bass_utils import run_bass_kernel_spmd

    nc = bacc.Bacc("TRN2", target_bir_lowering=False, num_devices=1)
    arrays, ins, outs = {}, {}, {}
    for name in _INS:
        a = np.ascontiguousarray(inputs[name])
        arrays[f"in_{name}"] = a
        ins[name] = nc.dram_tensor(f"in_{name}", a.shape, mybir.dt.from_np(a.dtype), kind="ExternalInput").ap()
    for name, shape in _OUTS:
        outs[name] = nc.dram_tensor(f"out_{name}", shape, F32, kind="ExternalOutput").ap()
    build(nc, ins, outs)
    r = run_bass_kernel_spmd(nc, [arrays], core_ids=[0])
    return tuple(r.results[0][f"out_{name}"] for name, _ in _OUTS)
```
